# Optimizing a Trainium2 kernel written in Bass

```python
import math
import jax, jax.numpy as jnp
from jax import lax
import numpy as np

D_MODEL = 1024
BATCH = 1
SEQ = 512
DEPTH = 2
DEC_BATCH = 8
DEC_SEQ = 8
PAST_LEN = 4096
PAGE_SIZE = 128

N_MIXERS = 2
N_A_LAYERS = (DEPTH + 1) // 2
N_B_LAYERS = DEPTH // 2
CHUNK = 128
D_GMLP = 3 * D_MODEL
G_A = 8
GW_A = D_GMLP // G_A
D_RNN = D_MODEL
H_B = 8
BW_B = D_RNN // H_B
CONV_W = 4
LRU_C = 8.0
D_FF = ((8 * D_MODEL + 3 * 256 - 1) // (3 * 256)) * 256
EPS = 1e-6

kernel_name = "hybrid_gmlp_rglru_decode_step"

def rms_norm(x, g):
    xf = x.astype(jnp.float32)
    y = xf * lax.rsqrt(jnp.mean(xf * xf, axis=-1, keepdims=True) + EPS)
    return (y * g.astype(jnp.float32)).astype(x.dtype)

def layer_norm(x, g, b):
    xf = x.astype(jnp.float32)
    mu = jnp.mean(xf, axis=-1, keepdims=True)
    xc = xf - mu
    y = xc * lax.rsqrt(jnp.mean(xc * xc, axis=-1, keepdims=True) + EPS)
    return (y * g.astype(jnp.float32) + b.astype(jnp.float32)).astype(x.dtype)

def gmlp_mixer(h, w_in, b_in, ln_g, ln_b, w_s, b_s, w_out):
    B, T, _ = h.shape
    z = jax.nn.gelu(h @ w_in + b_in)
    u, v = jnp.split(z, 2, axis=-1)
    v = layer_norm(v, ln_g, ln_b)
    n_chunks = -(-T // CHUNK)
    pad = n_chunks * CHUNK - T
    vp = jnp.pad(v, ((0, 0), (0, pad), (0, 0))).reshape(B, n_chunks, CHUNK, G_A, GW_A)
    mask = jnp.tril(jnp.ones((CHUNK, CHUNK), dtype=bool))
    ws = jnp.where(mask[None], w_s, jnp.zeros_like(w_s))
    mixed = jnp.einsum('gts,bcsge->bctge', ws, vp) + jnp.transpose(b_s)[None, None, :, :, None]
    mixed = mixed.reshape(B, n_chunks * CHUNK, D_GMLP)[:, :T]
    return (u * mixed) @ w_out, v

def _lin_comb(left, right):
    a_l, b_l = left
    a_r, b_r = right
    return a_l * a_r, a_r * b_l + b_r

def rglru_mixer(h, conv_hist, h0, w_in, conv_w, conv_b, w_a, b_a, w_x, b_x, lam, w_out):
    B, T, _ = h.shape
    y_br, x_br = jnp.split(h @ w_in, 2, axis=-1)
    gate = jax.nn.gelu(y_br)
    xpad = jnp.concatenate([conv_hist.astype(x_br.dtype), x_br], axis=1)
    xc = conv_b + sum(conv_w[k] * xpad[:, k:k + T] for k in range(CONV_W))
    new_hist = xpad[:, T:]
    xb = xc.reshape(B, T, H_B, BW_B)
    r = jax.nn.sigmoid(jnp.einsum('bthi,hij->bthj', xb, w_a) + b_a).reshape(B, T, D_RNN)
    i = jax.nn.sigmoid(jnp.einsum('bthi,hij->bthj', xb, w_x) + b_x).reshape(B, T, D_RNN)
    log_a = -LRU_C * r.astype(jnp.float32) * jax.nn.softplus(-lam.astype(jnp.float32))
    a = jnp.exp(log_a)
    mult = jnp.sqrt(-jnp.expm1(2.0 * log_a))
    b = mult * (i * xc).astype(jnp.float32)
    b = b.at[:, 0].add(a[:, 0] * h0.astype(jnp.float32))
    _, hs = lax.associative_scan(_lin_comb, (a, b), axis=1)
    out = (hs.astype(h.dtype) * gate) @ w_out
    return out, new_hist, hs[:, -1].astype(h.dtype)

def swiglu(h, w_in, w_out):
    g, u = jnp.split(h @ w_in, 2, axis=-1)
    return (jax.nn.silu(g) * u) @ w_out

def trunk(x, conv_hist, h0, norm_gains,
          gm_w_in, gm_b_in, gm_ln_g, gm_ln_b, gm_w_s, gm_b_s, gm_w_out,
          rg_w_in, rg_conv_w, rg_conv_b, rg_w_a, rg_b_a, rg_w_x, rg_b_x, rg_lambda, rg_w_out,
          ffn_w_in, ffn_w_out):
    new_conv, new_h, v_rows = [], [], []
    for li in range(DEPTH):
        g = norm_gains[li]
        hn = rms_norm(x, g[0])
        j = li // N_MIXERS
        if li % N_MIXERS == 0:
            m, v = gmlp_mixer(hn, gm_w_in[j], gm_b_in[j], gm_ln_g[j], gm_ln_b[j],
                              gm_w_s[j], gm_b_s[j], gm_w_out[j])
            v_rows.append(v)
        else:
            m, hist, hl = rglru_mixer(hn, conv_hist[j], h0[j], rg_w_in[j], rg_conv_w[j], rg_conv_b[j],
                                      rg_w_a[j], rg_b_a[j], rg_w_x[j], rg_b_x[j], rg_lambda[j], rg_w_out[j])
            new_conv.append(hist)
            new_h.append(hl)
        x = x + rms_norm(m, g[1])
        f = swiglu(rms_norm(x, g[2]), ffn_w_in[li], ffn_w_out[li])
        x = x + rms_norm(f, g[3])
    return x, jnp.stack(new_conv), jnp.stack(new_h), jnp.stack(v_rows)

def setup_inputs(seed: int = 0) -> dict:
    key = jax.random.key(seed)
    ks = jax.random.split(key, 24)
    f32 = jnp.float32
    nrm = lambda k, shape, scale: jax.random.normal(k, shape, f32) * scale
    u = jax.random.uniform(ks[20], (N_B_LAYERS, D_RNN), f32, 0.9, 0.999)
    s = u ** (1.0 / LRU_C)
    return {
        "x_prompt": nrm(ks[0], (BATCH, SEQ, D_MODEL), 1.0),
        "x_sample": nrm(ks[1], (DEC_BATCH, DEC_SEQ, D_MODEL), 1.0),
        "state_conv": nrm(ks[2], (N_B_LAYERS, DEC_BATCH, CONV_W - 1, D_RNN), 1.0),
        "state_h": nrm(ks[3], (N_B_LAYERS, DEC_BATCH, D_RNN), 1.0),
        "norm_gains": 1.0 + nrm(ks[4], (DEPTH, 4, D_MODEL), 0.02),
        "gm_w_in": nrm(ks[5], (N_A_LAYERS, D_MODEL, 2 * D_GMLP), D_MODEL ** -0.5),
        "gm_b_in": nrm(ks[6], (N_A_LAYERS, 2 * D_GMLP), 0.02),
        "gm_ln_g": 1.0 + nrm(ks[7], (N_A_LAYERS, D_GMLP), 0.02),
        "gm_ln_b": nrm(ks[8], (N_A_LAYERS, D_GMLP), 0.02),
        "gm_w_s": nrm(ks[9], (N_A_LAYERS, G_A, CHUNK, CHUNK), CHUNK ** -0.5),
        "gm_b_s": 1.0 + nrm(ks[10], (N_A_LAYERS, G_A, CHUNK), 0.02),
        "gm_w_out": nrm(ks[11], (N_A_LAYERS, D_GMLP, D_MODEL), D_GMLP ** -0.5),
        "rg_w_in": nrm(ks[12], (N_B_LAYERS, D_MODEL, 2 * D_RNN), D_MODEL ** -0.5),
        "rg_conv_w": nrm(ks[13], (N_B_LAYERS, CONV_W, D_RNN), CONV_W ** -0.5),
        "rg_conv_b": nrm(ks[14], (N_B_LAYERS, D_RNN), 0.02),
        "rg_w_a": nrm(ks[15], (N_B_LAYERS, H_B, BW_B, BW_B), BW_B ** -0.5),
        "rg_b_a": nrm(ks[16], (N_B_LAYERS, H_B, BW_B), 0.02),
        "rg_w_x": nrm(ks[17], (N_B_LAYERS, H_B, BW_B, BW_B), BW_B ** -0.5),
        "rg_b_x": nrm(ks[18], (N_B_LAYERS, H_B, BW_B), 0.02),
        "rg_lambda": jnp.log(s) - jnp.log1p(-s),
        "rg_w_out": nrm(ks[19], (N_B_LAYERS, D_RNN, D_MODEL), D_RNN ** -0.5),
        "ffn_w_in": nrm(ks[21], (DEPTH, D_MODEL, 2 * D_FF), D_MODEL ** -0.5),
        "ffn_w_out": nrm(ks[22], (DEPTH, D_FF, D_MODEL), D_FF ** -0.5),
    }

def reference(x_prompt, x_sample, state_conv, state_h, norm_gains,
              gm_w_in, gm_b_in, gm_ln_g, gm_ln_b, gm_w_s, gm_b_s, gm_w_out,
              rg_w_in, rg_conv_w, rg_conv_b, rg_w_a, rg_b_a, rg_w_x, rg_b_x, rg_lambda, rg_w_out,
              ffn_w_in, ffn_w_out):
    weights = (norm_gains, gm_w_in, gm_b_in, gm_ln_g, gm_ln_b, gm_w_s, gm_b_s, gm_w_out,
               rg_w_in, rg_conv_w, rg_conv_b, rg_w_a, rg_b_a, rg_w_x, rg_b_x, rg_lambda, rg_w_out,
               ffn_w_in, ffn_w_out)
    zero_conv = jnp.zeros((N_B_LAYERS, x_prompt.shape[0], CONV_W - 1, D_RNN), x_prompt.dtype)
    zero_h = jnp.zeros((N_B_LAYERS, x_prompt.shape[0], D_RNN), x_prompt.dtype)
    y_prompt, p_conv, p_h, _ = trunk(x_prompt, zero_conv, zero_h, *weights)
    y_sample, s_conv, s_h, s_v = trunk(x_sample, state_conv, state_h, *weights)
    return (y_prompt, y_sample, p_conv, p_h, s_conv, s_h, s_v)


_drawn_inputs = setup_inputs


def setup_inputs(seed=0):
    import zlib

    import numpy as np

    out = dict(_drawn_inputs(seed))
    spreads = {}
    factors = {'gm_ln_g': 2.826, 'gm_ln_b': 2.882, 'gm_b_s': 3.103, 'rg_b_a': 8.0, 'rg_b_x': 7.645}
    for name, (base, spread) in spreads.items():
        noise = np.random.default_rng([zlib.crc32(name.encode()), seed]).standard_normal(out[name].shape)
        drawn = base * np.exp(spread * noise) if base else spread * noise
        out[name] = __import__('jax').numpy.asarray(drawn.astype(out[name].dtype))
    for name, factor in factors.items():
        out[name] = (out[name] * factor).astype(out[name].dtype)
    return out
```

```python
from contextlib import ExitStack

import concourse.bass as bass
from concourse import mybir


F32 = mybir.dt.float32
F32R = mybir.dt.float32r
ALU = mybir.AluOpType
ACT = mybir.ActivationFunctionType

P = 128
EPS = 1e-6
BANK = 512


def plan(D, DG, DFF):
    counts = [("V", DG // 384 * 4), ("U", DG // P), ("GO", 2 * (DG // 256)), ("FI0", 2 * DFF // P),
              ("FO0", 2 * 12), ("RI", 2 * D // P), ("RO", 2 * (D // 256)), ("FI1", 2 * DFF // P),
              ("FO1", 2 * 12)]
    base, slots = {}, []
    for name, n in counts:
        base[name] = len(slots)
        for j in range(n):
            slots.append(j % 3 if name == "U" else len(slots) % 4)
    base["END"] = len(slots)
    return base, slots


def trunk_kernel(nc, x_prompt, x_sample, state_conv, state_h, norm_gains,
                 gm_w_in, gm_b_in, gm_ln_g, gm_ln_b, gm_w_s, gm_b_s, gm_w_out,
                 rg_w_in, rg_conv_w, rg_conv_b, rg_w_a, rg_b_a, rg_w_x, rg_b_x, rg_lambda, rg_w_out,
                 ffn_w_in, ffn_w_out,
                 y_prompt, y_sample, p_conv, p_h, s_conv, s_h, s_v):
    _, T, D = x_prompt.shape
    NB, NS, _ = x_sample.shape
    TS = NB * NS
    TT = T + TS
    HT = TT // 2
    KD = D // P
    DG = gm_w_out.shape[1]
    DFF = ffn_w_out.shape[1]
    GRP = gm_w_s.shape[1]
    GW = DG // GRP
    FG = GW // P
    KF = DFF // P
    CW = rg_conv_w.shape[1]
    NC = T // P
    NT = NC + 1
    assert TS == 64 and D == 1024 and GW == 384 and KF == 22 and CW == 4

    base, slot_of = plan(D, DG, DFF)

    def slot(n):
        return slot_of[n]

    def slot_free(n):
        return n - 2 if base["U"] <= n < base["GO"] + 3 else n - 3

    def landings(n):
        return sum(s == slot_of[n] for s in slot_of[:n + 1])

    with ExitStack() as ctx:
        def sb(name, shape, dt=F32):
            return ctx.enter_context(nc.sbuf_tensor(name, shape, dt))

        def sem(name):
            return ctx.enter_context(nc.semaphore(name))

        xT = sb("xT", [P, KD, TT])
        hh = sb("hh", [P, KD, TT], F32R)
        hl = sb("hl", [P, KD, TT], F32R)
        GSLOT = FG * TT
        ZW = NT * GW
        wide = sb("wide", [P, GSLOT + GRP * ZW])
        yb = sb("yb", [P, KD * TT])
        stage = sb("stage", [P, 4, 1024])
        whi = sb("whi", [P, 4, 1024], F32R)
        wlo = sb("wlo", [P, 4, 1024], F32R)
        acc = sb("acc", [P, NT * P])
        tmp = sb("tmp", [P, 3, TT])
        rb = sb("rb", [P, TT])
        par = sb("par", [P, 152])
        hist = sb("hist", [P, KD, 32])
        ident = sb("ident", [P, P])
        ones = sb("ones", [P, P])
        wsT = sb("wsT", [P, GRP, P])
        wsblk = sb("wsblk", [TS, GRP, TS])
        bsrow = sb("bsrow", [P, GRP, P])
        lnrow1 = sb("lnrow1", [P, 2 * GW])
        stats = sb("stats", [P, NT, GRP, 6])
        mv = sb("mv", [P, NT, 2])
        lnr = sb("lnr", [P, NT])
        std = sb("std", [P, NT])
        rtok = sb("rtok", [P, NT])
        epsc = sb("epsc", [P, 1])
        std_early = sb("std_early", [P, 1])
        sout = sb("sout", [P, KD, 36])
        hba = sb("hba", [P, KD])
        hbx = sb("hbx", [P, KD])
        sp2 = sb("sp2", [P, KD])
        spm4 = sb("spm4", [P, KD])
        spw = sb("spw", [P, 5, KD])
        s8 = sb("s8", [P, 2, NB])
        ps = ctx.enter_context(nc.psum_tensor("ps", [P, 8, BANK], F32))

        wideA = wide[:, :]
        psf = ps[:, :, :].rearrange("p b n -> p (b n)")
        def TOK(q):
            return ps[:, 0, HT:HT + NT] if q % 2 else ps[:, 7, HT:HT + NT]

        BC = psf[:, 6 * BANK:6 * BANK + TT]
        diag = tmp[:, :, :].rearrange("p a n -> p (a n)")[:, 0:NT * P]

        def bc3(ap2, n):
            return ap2.unsqueeze(2).to_broadcast([ap2.shape[0], ap2.shape[1], n])

        def halves(ap2):
            return ap2.rearrange("p (h n) -> p h n", h=2)

        def pair(m, lo=0, hi=HT):
            return ps[:, 2 * m:2 * m + 2, lo:hi]

        def wtile(k):
            return wideA[:, bass.ds(k * TT, TT)]

        def yt(k):
            return yb[:, bass.ds(k * TT, TT)]

        def z(g, t):
            rows = P if t < NC else TS
            return wide[0:rows, bass.ds(g * ZW + (GSLOT + t * GW), GW)]

        xin = [wide[0:(P if c < NC else TS), c * D:(c + 1) * D] for c in range(NT)]
        RAW0 = GSLOT + GRP * ZW - 2 * P - D
        praw1 = wide[0:88, RAW0:RAW0 + P]
        praw2 = wide[0:64, RAW0 + P:RAW0 + 2 * P]
        sraw = wide[0:32, RAW0 + 2 * P:RAW0 + 2 * P + D]
        brow = yb[:, 0:DG]
        wraw = yb[:, DG:DG + GRP * P].rearrange("p (g s) -> p g s", g=GRP)
        vbuf = [yb[:, ZW * b:ZW * (b + 1)].rearrange("p (t e) -> p t e", t=NT) for b in range(2)]
        lnrow = [yb[:, 2 * ZW:2 * ZW + 2 * GW], lnrow1[:, :]]
        XB = T + CW - 1 + NB * (NS + CW - 1)
        XBP = T + CW - 1
        XC0 = KD * XB
        GATE0 = XC0 + KD * TT
        WG0 = GATE0 + KD * TT
        assert WG0 + 2 * KD * P <= GSLOT + GRP * ZW

        def xb_p(h, k, n=T):
            return wide[:, h * XB + k:h * XB + k + n]

        def xb_s(h):
            return wide[:, h * XB + XBP:(h + 1) * XB].rearrange("p (b t) -> p b t", b=NB)

        def xbt(h):
            return wide[:, h * XB:h * XB + TT]

        def xc(h):
            return wide[:, XC0 + h * TT:XC0 + (h + 1) * TT]

        def gate(h):
            return wide[:, GATE0 + h * TT:GATE0 + (h + 1) * TT]

        def wg(mat, h):
            return wide[:, WG0 + (mat * KD + h) * P:WG0 + (mat * KD + h + 1) * P]

        def gain(layer, i, k):
            c = (layer * 4 + i) * KD + k
            return par[:, c:c + 1]

        BIN0, CVW0, CVB0, BA0, BX0, LAM0 = 64, 88, 120, 128, 136, 144

        landed = [sem(f"weights_landed{s}") for s in range(4)]
        hi_ready = sem("weights_hi_ready")
        lo_ready = sem("weights_lo_ready")
        unit_done = sem("unit_done")
        pair_free = [sem(f"pair_free{m}") for m in range(4)]
        h_pair_used = sem("h_pair_used")
        a_hi = sem("wide_hi_ready")
        a_lo = sem("wide_lo_ready")
        h_hi = sem("h_hi_ready")
        h_lo = sem("h_lo_ready")
        par1_landed = sem("par1_landed")
        par2_landed = sem("par2_landed")
        x_landed = sem("x_landed")
        xs_landed = sem("x_sample_landed")
        ws_landed = sem("ws_landed")
        brow_landed = sem("brow_landed")
        bs_landed = sem("bs_landed")
        lnrow_landed = [sem("lnrow_landed0"), sem("lnrow_landed1")]
        v_stored = [sem("v_stored0"), sem("v_stored1")]
        wg_landed = sem("gate_weights_landed")
        blk_landed = sem("wsblk_landed")
        consts = sem("consts_ready")
        par1_turned, par1_ready = sem("par1_turned"), sem("par1_ready")
        par2_turned, par2_ready = sem("par2_turned"), sem("par2_ready")
        x_turned, x_ready = sem("x_turned"), sem("x_ready")
        ws_masked, ws_turned, ws_ready = sem("ws_masked"), sem("ws_turned"), sem("ws_ready")
        sq_ready, sq_added = sem("squares_ready"), sem("squares_added")
        tok_done, std_ready, diag_ready = sem("tok_done"), sem("std_ready"), sem("diag_ready")
        rtok_ready = sem("rtok_ready")
        bc_done, rb_ready = sem("bc_done"), sem("rb_ready")
        v_tile_done, z_evicted, z_act = sem("v_tile_done"), sem("z_evicted"), sem("z_activated")
        z_stats, var_ready, lnstd_ready, ln_ready = sem("z_stats"), sem("var_ready"), sem("lnstd_ready"), sem("lnr_ready")
        ln_half, ln_done = sem("ln_half"), sem("ln_done")
        mix_done = sem("mix_done")
        u_act = sem("u_activated")
        gated = sem("gated")
        y_tile_done, y_sq = sem("y_tile_done"), sem("y_squared")
        t_ready, x0_ready, res_ready = sem("t_ready"), sem("residual0_ready"), sem("residual_ready")
        f_act = sem("g_activated")
        ffn_gated = sem("ffn_gated")
        sp_chain, sp_exp, sp_ready = sem("sp_chain"), sem("sp_exp"), sem("sp_ready")
        hb_ready = sem("half_bias_ready")
        pads_ready = sem("pads_ready")
        tap0, tap_chain, conv_done, tails = sem("tap0"), sem("tap_chain"), sem("conv_done"), sem("tails_saved")
        t2_ready, p1_ready = sem("t2_ready"), sem("p1_ready")
        a_ready, sqrt_ready = sem("a_ready"), sem("sqrt_ready")
        p1s_ready, b_ready, seq_ready = sem("p1s_ready"), sem("b_ready"), sem("sequences_ready")
        pool_chain = sem("pool_chain")
        scanned, rg_gated = sem("scanned"), sem("rg_gated")
        y_act = sem("y_activated")
        gates_done = sem("gates_done")
        x_last = [sem("x_last_even"), sem("x_last_odd")]
        out_turned, out_stored = sem("out_turned"), sem("out_stored")
        out_act, out_dve = sem("out_copied_by_act"), sem("out_copied_by_dve")
        so_turned, so_copied = sem("so_turned"), sem("so_copied")

        free0 = {}
        count = [0, 0, 0, 0]
        for name, add in (("U", (GRP, GRP, GRP, DG // P)), ("GO", (2,) * 4), ("FI0", (KF // 2,) * 4),
                          ("FO0", (2,) * 4), ("RI", (8,) * 4), ("RO", (2,) * 4), ("FI1", (KF // 2,) * 4),
                          ("FO1", (2,) * 4)):
            free0[name] = list(count)
            count = [a + b for a, b in zip(count, add)]
        free0["END"] = list(count)

        NORM = {"V": 0, "GO": 1, "FI0": 2, "FO0": 3, "RI": 4, "RO": 5, "FI1": 6, "FO1": 7}
        pair3_used = {1: free0["FI0"][3], 3: free0["RI"][3], 5: free0["FI1"][3], 7: free0["END"][3]}
        HSET = {"V": 0, "FI0": 1, "RI": 2, "FI1": 3}
        USED = {"GO": 0, "FO0": 1, "RO": 2, "FO1": 3}
        AB = {"GO": 0, "FO0": 24, "RO": 48, "FO1": 56}
        KO = {"GO": DG // P, "FO0": KF, "RO": KD, "FO1": KF}

        def out_units(name):
            k = KO[name]
            if k % 4 == 0:
                return [(j, 2) for j in range(0, k, 2)]
            return [(j, 2) for j in range(0, k - 2, 2)] + [(k - 2, 1), (k - 1, 1)]

        OUT_BANK = [0, 1, 2, 3, 6, 4, 5, 7, 0, 1]

        def out_by_act(b):
            return b < NT or b % 2 == 1

        def out_tile(b):
            hf, c = divmod(b, NT)
            return xin[c][:, hf * 4 * P:(hf + 1) * 4 * P]

        def out_bank(b):
            return ps[0:P if b % NT < NC else TS, OUT_BANK[b], :]

        block = ctx.enter_context(nc.Block())

        @block.sync
        def _(sp):
            def load(n, src, width, shape, i=0, per=0):
                dst = stage[:, slot(n), 0:width].rearrange("p (k c) -> p k c", c=shape)
                if n >= 4:
                    sp.wait_ge(lo_ready, i * per + slot_free(n))
                sp.dma_start(dst, src).then_inc(landed[slot(n)], 16)

            def rows(w, r0, nk, c0, width):
                return w[r0:r0 + nk * P, bass.ds(c0, width)].rearrange("(k p) c -> p k c", p=P)

            sp.dma_start(praw1[0:64], norm_gains.rearrange("l i (k p) -> (l i k) p", p=P)).then_inc(par1_landed, 16)
            sp.dma_start(praw1[64:88], gm_b_in[0, 0:DG].rearrange("(k p) -> k p", p=P)).then_inc(par1_landed, 16)
            sp.dma_start(xin[NC], x_sample.rearrange("b t d -> (b t) d")).then_inc(xs_landed, 16)
            for c in range(NC):
                sp.dma_start(xin[c], x_prompt[0, c * P:(c + 1) * P, :]).then_inc(x_landed, 16)
            wv = gm_w_in[0]
            for n in range(4):
                load(n, rows(wv, 2 * P * n, 2, DG, GW), 2 * GW, GW)
            sp.dma_start(brow, gm_b_in[0, DG:2 * DG].partition_broadcast(P)).then_inc(brow_landed, 16)
            for j, (v, r) in enumerate(((rg_conv_w[0], 32), (rg_conv_b, 8), (rg_b_a[0], 8), (rg_b_x[0], 8), (rg_lambda, 8))):
                at = (0, 32, 40, 48, 56)[j]
                src = v if j in (2, 3) else v.rearrange("w (k p) -> (w k) p", p=P)
                sp.dma_start(praw2[at:at + r], src).then_inc(par2_landed, 16)
            sp.dma_start(sraw[0:24], state_conv[0].rearrange("b w d -> (b w) d")).then_inc(par2_landed, 16)
            sp.dma_start(sraw[24:32], state_h[0]).then_inc(par2_landed, 16)
            sp.dma_start(wraw, gm_w_s[0].rearrange("g t s -> t g s")).then_inc(ws_landed, 16)
            sp.dma_start(bsrow[:, :, :], gm_b_s[0].partition_broadcast(P)).then_inc(bs_landed, 16)
            with sp.Fori(0, GRP - 1) as i:
                c0 = sp.snap(i * GW + (DG + GW))
                seen = [sp.snap(i * 4 + slot_free(4 + j)) for j in range(4)]
                for j in range(4):
                    sp.wait_ge(lo_ready, seen[j])
                    sp.dma_start(stage[:, slot(4 + j), 0:2 * GW].rearrange("p (k c) -> p k c", c=GW),
                                 rows(wv, 2 * P * j, 2, c0, GW)).then_inc(landed[slot(4 + j)], 16)

            def in_phase(first, w, col, iters, per):
                with sp.Fori(0, iters) as i:
                    cols = [sp.snap(col(i, c)) for c in range(per)]
                    seen = [sp.snap(i * per + slot_free(first + c)) for c in range(per)]
                    for c in range(per):
                        sp.wait_ge(lo_ready, seen[c])
                        sp.dma_start(stage[:, slot(first + c), :].rearrange("p (k c) -> p k c", c=P),
                                     rows(w, 0, KD, cols[c], P)).then_inc(landed[slot(first + c)], 16)

            def out_phase(name, w):
                units = out_units(name)
                first, per = base[name], len(units)
                with sp.Fori(0, 2) as i:
                    c0 = sp.snap(i * (4 * P))
                    seen = [sp.snap(i * per + slot_free(first + j)) for j in range(per)]
                    for j, (k, nk) in enumerate(units):
                        sp.wait_ge(lo_ready, seen[j])
                        sp.dma_start(stage[:, slot(first + j), 0:nk * 4 * P].rearrange("p (k c) -> p k c", c=4 * P),
                                     rows(w, k * P, nk, c0, 4 * P)).then_inc(landed[slot(first + j)], 16)

            def ffn_col(i, c):
                return i * (2 * P) + (c * P if c < 2 else DFF + (c - 2) * P)

            in_phase(base["U"], wv, lambda i, c: i * (6 * P) + c * P, GRP // 2, 6)
            out_phase("GO", gm_w_out[0])
            in_phase(base["FI0"], ffn_w_in[0], ffn_col, KF // 2, 4)
            out_phase("FO0", ffn_w_out[0])
            sp.wait_ge(a_lo, AB["RO"])
            for m, w in enumerate((rg_w_a, rg_w_x)):
                sp.dma_start(wide[:, WG0 + m * KD * P:WG0 + (m + 1) * KD * P].rearrange("p (h j) -> p h j", h=KD),
                             w[0].rearrange("h i j -> i h j")).then_inc(wg_landed, 16)
            in_phase(base["RI"], rg_w_in[0], lambda i, c: i * (4 * P) + (D + c * P), 2, 4)
            in_phase(base["RI"] + KD, rg_w_in[0], lambda i, c: i * (4 * P) + c * P, 2, 4)
            out_phase("RO", rg_w_out[0])
            in_phase(base["FI1"], ffn_w_in[1], ffn_col, KF // 2, 4)
            out_phase("FO1", ffn_w_out[1])
            sp.wait_ge(so_copied, 1)
            st = wide[0:36, NT * D:(NT + 1) * D]
            sp.dma_start(p_conv[0, 0], st[0:3]).then_inc(out_stored, 16)
            sp.dma_start(s_conv[0].rearrange("b w d -> (b w) d"), st[3:27]).then_inc(out_stored, 16)
            sp.dma_start(p_h[0], st[27:28]).then_inc(out_stored, 16)
            sp.dma_start(s_h[0], st[28:36]).then_inc(out_stored, 16)
            for b in range(2 * NT):
                hf, c = divmod(b, NT)
                on_act = out_by_act(b)
                sp.wait_ge(out_act if on_act else out_dve, sum(out_by_act(x) == on_act for x in range(b + 1)))
                dst = y_prompt[0, c * P:(c + 1) * P, :] if c < NC else y_sample.rearrange("b t d -> (b t) d")
                sp.dma_start(dst[:, hf * 4 * P:(hf + 1) * 4 * P], out_tile(b)).then_inc(out_stored, 16)
            sp.wait_ge(out_stored, 16 * (4 + 2 * NT))
            for b in range(2):
                sp.wait_ge(v_stored[b], 16 * (GRP // 2))

        @block.tensor
        def _(pe):
            def mm(out, w, x, start, stop):
                return pe.matmul(out, w, x, start=start, stop=stop)

            def three(m, hi_w, lo_w, k, first, last):
                a, b = ps[:, 2 * m, 0:HT], ps[:, 2 * m + 1, 0:HT]
                mm(a, hi_w, hh[:, k, 0:HT], first, False)
                mm(b, hi_w, hh[:, k, HT:TT], first, False)
                mm(a, hi_w, hl[:, k, 0:HT], False, False)
                mm(b, hi_w, hl[:, k, HT:TT], False, False)
                mm(a, lo_w, hh[:, k, 0:HT], False, last)
                return mm(b, lo_w, hh[:, k, HT:TT], False, last)

            def token_sums(q):
                for c in range(NT):
                    if c in (0, 2):
                        pe.wait_ge(sq_added, 8 * q + (7 if c == 0 else 8))
                    last = mm(TOK(q)[:, c:c + 1], acc[:, c * P:(c + 1) * P], ones[:, 0:1], True, True)
                last.then_inc(tok_done, 1)

            def spread(q):
                pe.wait_ge(diag_ready, q + 1)
                if q % 2:
                    pe.wait_ge(pair_free[3], pair3_used[q])
                mm(BC[:, 0:T], ones[:, :], diag[:, 0:T], True, True)
                mm(BC[:, T:TT], ones[0:TS, :], diag[0:TS, T:TT], True, True).then_inc(bc_done, 1)

            pe.wait_ge(consts, 3)
            pe.wait_ge(par1_landed, 32)
            pe.transpose(ps[:, 0, 0:88], praw1, ident[0:88, 0:88]).then_inc(par1_turned, 1)
            pe.wait_ge(xs_landed, 16)
            for k in range(KD):
                last = pe.transpose(ps[:, 7, k * TS:(k + 1) * TS], xin[NC][:, k * P:(k + 1) * P], ident[0:TS, 0:TS])
            last.then_inc(x_turned, 1)
            pe.wait_ge(x_landed, 16 * NC)

            def turn_x(k):
                if k >= 2:
                    pe.wait_ge(x_ready, k)
                for c in range(NC):
                    last = pe.transpose(ps[:, 5 + k % 2, c * P:(c + 1) * P], xin[c][:, k * P:(k + 1) * P], ident[:, :])
                last.then_inc(x_turned, 1)

            turn_x(0)
            turn_x(1)

            def v_group(g, first, i=0):
                for j in range(4):
                    n = 4 * g + j
                    pe.wait_ge(lo_ready, i * 4 + (n + 1))
                    for kk in range(2):
                        k = 2 * j + kk
                        if first:
                            if k + 2 < KD:
                                turn_x(k + 2)
                            pe.wait_ge(h_lo, k + 1)
                        wh = whi[:, slot(n), kk * GW:(kk + 1) * GW]
                        wl = wlo[:, slot(n), kk * GW:(kk + 1) * GW]
                        for t in range(NT):
                            if k == KD - 1 and first and t == 1:
                                token_sums(0)
                            if k == 0 and first and t == 0:
                                pe.wait_ge(par1_ready, 1)
                            if k == 0 and not first:
                                pe.wait_ge(z_evicted, i * NT + (NT * (g - 1) + t + 1))
                            r = P if t < NC else TS
                            o = ps[0:r, t, 0:GW]
                            c = slice(t * P, t * P + r)
                            mm(o, hh[:, k, c], wh, k == 0, False)
                            mm(o, hl[:, k, c], wh, False, False)
                            last = mm(o, hh[:, k, c], wl, False, k == KD - 1)
                            if k == KD - 1 and t < NC:
                                last.then_inc(v_tile_done, 1)
                    last.then_inc(unit_done, 1)

            v_group(0, True)
            v_group(1, False)
            spread(0)
            pe.wait_ge(ws_masked, 1)
            for g in range(GRP):
                at = 4 * BANK + BANK + g * P if g < 4 else 6 * BANK + g * P - 4 * P
                if g == 4:
                    pe.wait_ge(rb_ready, 1)
                last = pe.transpose(psf[:, at:at + P], wraw[:, g, :], ident[:, :])
                if g == 3:
                    last.then_inc(ws_turned, 1)
            last.then_inc(ws_turned, 1)
            v_group(2, False)
            pe.wait_ge(ws_ready, 2)
            pe.wait_ge(par2_landed, 16 * 7)
            pe.transpose(ps[:, 5, 0:64], praw2, ident[0:64, 0:64])
            for k in range(KD):
                last = pe.transpose(ps[:, 5, 64 + 32 * k:96 + 32 * k], sraw[:, k * P:(k + 1) * P], ident[0:32, 0:32])
            last.then_inc(par2_turned, 1)
            with pe.Fori(0, GRP - 3) as i:
                v_group(3, False, i)

            def mix(x, f, b, g):
                pe.wait_ge(pair_free[3], x)
                for c in range(NC):
                    mm(ps[:, 6, c * P:(c + 1) * P], vbuf[b][:, c, f * P:(f + 1) * P],
                       wsT[:, bass.ds(g, 1), :].rearrange("p a t -> p (a t)"), True, True)
                mm(ps[:, 7, 0:TS], vbuf[b][0:TS, NC, f * P:(f + 1) * P],
                   wsblk[:, bass.ds(g, 1), :].rearrange("p a t -> p (a t)"), True, True).then_inc(mix_done, 1)

            def u_body(i, first=False, last_body=False):
                for c in range(6):
                    n = base["U"] + c
                    m = c % 3
                    pe.wait_ge(lo_ready, i * 6 + (n + 1))
                    if first and c < 3:
                        pe.wait_ge(z_evicted, NT * (GRP - 1) + min(2 * c + 2, NT))
                    else:
                        pe.wait_ge(pair_free[m], i * 2 + (c // 3))
                    for k in range(KD):
                        at = three(m, whi[:, slot(n), k * P:(k + 1) * P], wlo[:, slot(n), k * P:(k + 1) * P],
                                   k, k == 0, k == KD - 1)
                        if last_body and c == 5 and k % 2 and k < KD - 1:
                            at.then_inc(h_pair_used, 1)
                    at.then_inc(unit_done, 1)
                    if first and c < 2:
                        continue
                    if c % 3 == 2:
                        pe.wait_ge(ln_done, i * (2 * NT) + (c // 3 + 1) * NT)
                    gshift, f = divmod(c - 2, 3)
                    if first and c == 2:
                        pe.wait_ge(blk_landed, 16 * NB)
                        pe.wait_ge(rb_ready, 1)
                    mix(i * 6 + (c - 2), f, gshift % 2, i * 2 + gshift)

            u_body(0, first=True)
            with pe.Fori(1, GRP // 2 - 1) as i:
                u_body(i)
            u_body(GRP // 2 - 1, last_body=True)
            for x in (DG // P - 2, DG // P - 1):
                mix(x, x % FG, (x // FG) % 2, x // FG)

            def out_phase(name):
                units = out_units(name)
                first, per = base[name], len(units)
                with pe.Fori(0, 2) as i:
                    def part(j, kk, m):
                        k, at = units[j][0] + kk, kk * 4 * P + m * P
                        return three(m, whi[:, slot(first + j), at:at + P], wlo[:, slot(first + j), at:at + P],
                                     2 * (j % 4) + kk, k == 0, k == KO[name] - 1)

                    for j in range(per - 2):
                        pe.wait_ge(lo_ready, i * per + (first + j + 1))
                        pe.wait_ge(a_lo, i * per + (AB[name] + j + 1))
                        for kk in range(units[j][1]):
                            for m in range(4):
                                if j == 0 and kk == 0:
                                    pe.wait_ge(pair_free[m], i + free0[name][m])
                                last = part(j, kk, m)
                        last.then_inc(unit_done, 1)
                    pe.wait_ge(lo_ready, i * per + (first + per))
                    pe.wait_ge(a_lo, i * per + (AB[name] + per))
                    for m in range(4):
                        for j in (per - 2, per - 1):
                            for kk in range(units[j][1]):
                                last = part(j, kk, m)
                            if m == 3:
                                last.then_inc(unit_done, 1)
                        if m < 3:
                            last.then_inc(y_tile_done, 1)
                token_sums(NORM[name])
                spread(NORM[name])

            def first_tiles(name):
                n, q, h0 = base[name], NORM[name], KD * HSET[name]

                def part(m, k):
                    return three(m, whi[:, slot(n + m), k * P:(k + 1) * P], wlo[:, slot(n + m), k * P:(k + 1) * P],
                                 k, k == 0, k == KD - 1)

                pe.wait_ge(h_hi, h0 + 1)
                for m in range(3):
                    pe.wait_ge(lo_ready, n + m + 1)
                    pe.wait_ge(pair_free[m], free0[name][m])
                    for w in (whi, wlo):
                        for j in range(2):
                            mm(ps[:, 2 * m + j, 0:HT], w[:, slot(n + m), 0:P], hh[:, 0, j * HT:(j + 1) * HT], w is whi, False)
                pe.wait_ge(h_lo, h0 + 1)
                for m in range(3):
                    for j in range(2):
                        mm(ps[:, 2 * m + j, 0:HT], whi[:, slot(n + m), 0:P], hl[:, 0, j * HT:(j + 1) * HT], False, False)
                for k in range(1, KD):
                    pe.wait_ge(h_lo, h0 + k + 1)
                    for m in range(2):
                        last = part(m, k)
                        if k == KD - 1:
                            last.then_inc(unit_done, 1)
                    if k < KD - 3:
                        part(2, k)
                token_sums(q)
                for k in range(KD - 3, KD):
                    last = part(2, k)
                last.then_inc(unit_done, 1)
                spread(q)
                pe.wait_ge(rb_ready, q + 1)
                tile_unit(n + 3, 3, free0[name][3], last_unit=False)

            def tile_unit(n, m, freed, last_unit, i=0, per=0):
                pe.wait_ge(lo_ready, i * per + (n + 1))
                pe.wait_ge(pair_free[m], freed)
                for k in range(KD):
                    last = three(m, whi[:, slot(n), k * P:(k + 1) * P], wlo[:, slot(n), k * P:(k + 1) * P],
                                 k, k == 0, k == KD - 1)
                    if last_unit and k % 2 and k < KD - 1:
                        last.then_inc(h_pair_used, 1)
                last.then_inc(unit_done, 1)

            def ffn_in(name):
                first_tiles(name)
                nb = KF // 2
                with pe.Fori(1, nb - 1) as i:
                    for c in range(4):
                        tile_unit(base[name] + c, c, i + free0[name][c], False, i, 4)
                for c in range(4):
                    tile_unit(base[name] + 4 * (nb - 1) + c, c, nb - 1 + free0[name][c], c == 3)

            out_phase("GO")
            ffn_in("FI0")
            out_phase("FO0")

            first_tiles("RI")
            f0 = free0["RI"]
            for u in range(4, 9):
                tile_unit(base["RI"] + u, u % 4, f0[u % 4] + u // 4, False)
            pe.wait_ge(wg_landed, 32)
            e = 9
            for mat in range(2):
                for h in range(KD):
                    if mat == 0:
                        pe.wait_ge(conv_done, h + 1)
                    pe.wait_ge(pair_free[e % 4], f0[e % 4] + e // 4)
                    for half in range(2):
                        last = mm(ps[:, 2 * (e % 4) + half, 0:HT], wg(mat, h), xc(h)[:, half * HT:(half + 1) * HT], True, True)
                    last.then_inc(gates_done, 1)
                    e += 1
            for u in range(9, 16):
                tile_unit(base["RI"] + u, e % 4, f0[e % 4] + e // 4, u == 15)
                e += 1

            out_phase("RO")
            ffn_in("FI1")
            out_phase("FO1")

            for k in range(KD):
                last = pe.transpose(ps[0:36, 4 + k // 4, (k % 4) * P:(k % 4 + 1) * P], sout[:, k, :], ident[:, :])
            last.then_inc(so_turned, 1)
            for k in range(KD):
                pe.wait_ge(x_last[k % 2], k // 2 + 1)
                if k == 4:
                    pe.wait_ge(so_copied, 1)
                    pe.wait_ge(out_act, 2)
                for c in range(NT):
                    r = P if c < NC else TS
                    if k == 0 and c == NC:
                        pe.wait_ge(rb_ready, NORM["FO1"] + 1)
                    last = pe.transpose(out_bank(c + NT * (k // 4))[:, (k % 4) * P:(k % 4 + 1) * P],
                                        xT[:, k, c * P:c * P + r], ident[:, :])
                    if k % 4 == 3:
                        last.then_inc(out_turned, 1)

        @block.scalar
        def _(act):
            def split_hi(n, width=1024, i=0, per=0):
                s = slot(n)
                turns = {0: 0, 4: 1, 6: 2}[per]
                act.wait_ge(landed[s], i * (16 * turns) + 16 * landings(n))
                if n >= 4:
                    act.wait_ge(unit_done, i * per + slot_free(n))
                act.activation(whi[:, s, 0:width], stage[:, s, 0:width], ACT.Copy).then_inc(hi_ready, 1)

            def width_of(n):
                for name in ("FO0", "FO1"):
                    if base[name] <= n < base[name] + 24 and (n - base[name]) % 12 >= 10:
                        return 512
                return 1024

            def std_of(q):
                act.wait_ge(tok_done, q + 1)
                act.activation(std[:, :], TOK(q), ACT.Sqrt, scale=1.0 / D, bias=epsc[:, 0:1]).then_inc(std_ready, 1)

            def rb_of(q):
                act.wait_ge(bc_done, q + 1)
                if q % 2:
                    act.wait_ge(t_ready, KD * (q // 2) + 1)
                act.activation(rb[:, :], BC, ACT.Copy).then_inc(rb_ready, 1)

            def square(q, r, src):
                if r >= 4:
                    act.wait_ge(sq_added, 8 * q + r - 3)
                dst = tmp[:, r % 3, :] if r else acc[:, 0:TT]
                if r < KD - 1:
                    act.activation(halves(dst), src(0, 2), ACT.Square).then_inc(sq_ready, 1)
                else:
                    for j in range(2):
                        act.activation(halves(dst)[:, j:j + 1, :], src(j, j + 1), ACT.Square).then_inc(sq_ready, 1)

            def h_tile(q, k, layer, i):
                act.activation(hh[:, k, :], xT[:, k, :], ACT.Copy, scale=gain(layer, i, k)).then_inc(h_hi, 1)
                square(q, k, lambda lo, hi: halves(xT[:, k, :])[:, lo:hi, :])

            def source(name, k, nk):
                if name == "RO":
                    return wide[:, GATE0 + k * TT:GATE0 + (k + nk) * TT]
                return wide[:, k * TT:(k + nk) * TT]

            def wide_hi(name, s):
                units = out_units(name)
                j = s % len(units)
                k, nk = units[j]
                act.wait_ge({"GO": gated, "RO": rg_gated}.get(name, ffn_gated),
                            k + nk + (KF if name == "FO1" else 0))
                if s < 3:
                    act.wait_ge(h_pair_used, 3 * USED[name] + s + 1)
                else:
                    act.wait_ge(unit_done, base[name] + max(s - 3, 0))
                at = 2 * (j % 4)
                act.activation(hh[:, at:at + nk, :].rearrange("p k n -> p (k n)"), source(name, k, nk),
                               ACT.Copy).then_inc(a_hi, 1)

            act.wait_ge(par1_turned, 1)
            act.activation(par[:, 0:88], ps[:, 0, 0:88], ACT.Copy).then_inc(par1_ready, 1)
            split_hi(0, 2 * GW)
            split_hi(1, 2 * GW)
            act.wait_ge(par1_ready, 1)
            act.wait_ge(consts, 3)
            act.activation(std_early[:, :], epsc[:, :], ACT.Sqrt)
            for k in range(KD):
                act.wait_ge(x_ready, k + 2)
                h_tile(0, k, 0, 0)
                if k in (2, 4):
                    split_hi(1 + k // 2, 2 * GW)
            std_of(0)

            def v_gelu(g, i=0):
                for t in range(NT):
                    act.wait_ge(z_evicted, i * NT + (NT * g + t + 1))
                    zt = z(i + g, t)
                    act.activation(zt, zt, ACT.Gelu_apprx_tanh).then_inc(z_act, 1)

            def v_group(g, i=0, last=False):
                for j in range(4):
                    split_hi(4 * g + j + 2, 1024 if last and j >= 2 else 2 * GW, i, 0 if last or g < 3 else 4)
                v_gelu(g, i)

            split_hi(4, 2 * GW)
            split_hi(5, 2 * GW)
            v_gelu(0)
            v_group(1)
            rb_of(0)
            for half in range(2):
                act.wait_ge(ws_turned, half + 1)
                act.activation(wsT[:, 4 * half:4 * half + 4, :].rearrange("p g t -> p (g t)"),
                               ps[:, 5 + half, :], ACT.Copy).then_inc(ws_ready, 1)
            v_group(2)
            act.wait_ge(par2_turned, 1)
            act.activation(par[:, 88:152], ps[:, 5, 0:64], ACT.Copy)
            act.activation(hist[:, :, :].rearrange("p k c -> p (k c)"), ps[:, 5, 64:320], ACT.Copy).then_inc(par2_ready, 1)
            act.wait_ge(sp_chain, 2)
            act.activation(spw[:, 2, :], spw[:, 1, :], ACT.Exp, scale=-1.0).then_inc(sp_exp, 1)
            with act.Fori(0, GRP - 4) as i:
                v_group(3, i)
            v_group(GRP - 1, last=True)
            act.wait_ge(var_ready, 1)
            act.activation(lnr[:, 0:NC], mv[:, 0:NC, 1], ACT.Sqrt, bias=epsc[:, 0:1])
            act.activation(lnr[0:TS, NC:NT], mv[0:TS, NC, 1:2], ACT.Sqrt, bias=epsc[0:TS, 0:1]).then_inc(lnstd_ready, 1)

            def u_body(i, last=False):
                for c in range(6):
                    m = c % 3
                    split_hi(base["U"] + c + 2, 1024, i, 6)
                    if last and c == 5:
                        wide_hi("GO", 0)
                        wide_hi("GO", 1)
                    act.wait_ge(pair_free[m], i * 2 + (c // 3 + 1))
                    act.activation(tmp[:, m, :], tmp[:, m, :], ACT.Gelu_apprx_tanh,
                                   bias=par[:, bass.ds(i * 6 + (BIN0 + c), 1)]).then_inc(u_act, 1)

            with act.Fori(0, GRP // 2 - 1) as i:
                u_body(i)
            u_body(GRP // 2 - 1, last=True)

            def out_phase(name):
                units = out_units(name)
                per, q = len(units), NORM[name]
                for s in range(2 * per):
                    n = base[name] + s
                    if n + 2 < base["END"]:
                        split_hi(n + 2, width_of(n + 2))
                    if s + 2 < 2 * per:
                        wide_hi(name, s + 2)
                    if s % per == per - 1:
                        G = s // per
                        if name == "GO" and G == 0:
                            for b in range(2):
                                act.wait_ge(v_stored[b], 16 * (GRP // 2))
                        for m in range(4):
                            if m < 3:
                                act.wait_ge(y_tile_done, 6 * USED[name] + 3 * G + m + 1)
                            else:
                                if G:
                                    act.activation(std_early[:, :], epsc[:, :], ACT.Sqrt)
                                act.wait_ge(unit_done, n + 1)
                            square(q, 4 * G + m, lambda lo, hi: ps[:, 2 * m + lo:2 * m + hi, 0:HT])
                            act.activation(halves(yt(4 * G + m)), pair(m), ACT.Copy).then_inc(pair_free[m], 1)
                std_of(q)
                if base[name] + 2 * per < base["END"]:
                    split_hi(base[name] + 2 * per + 2)
                rb_of(q)

            def first_tiles(name, layer, i):
                q, n = NORM[name], base[name]
                for k in range(KD):
                    if k == 0:
                        act.wait_ge(x0_ready, HSET[name])
                    else:
                        act.wait_ge(res_ready, (KD - 1) * (HSET[name] - 1) + k)
                    h_tile(q, k, layer, i)
                std_of(q)
                split_hi(n + 3)
                rb_of(q)

            def silu(name, i, c):
                act.wait_ge(pair_free[c], i + (free0[name][c] + 1))
                w = wtile(i * 2 + c)
                act.activation(w, w, ACT.Silu).then_inc(f_act, 1)

            def ffn_in(name, layer, out):
                first_tiles(name, layer, 2)
                n, nb = base[name], KF // 2
                silu(name, 0, 0)
                silu(name, 0, 1)
                split_hi(n + 4)
                split_hi(n + 5)
                with act.Fori(1, nb - 1) as i:
                    for c in range(4):
                        split_hi(n + c + 2, 1024, i, 4)
                        if c < 2:
                            silu(name, i, c)
                for c in range(4):
                    split_hi(n + 4 * (nb - 1) + c + 2)
                    if c < 2:
                        silu(name, nb - 1, c)
                wide_hi(out, 0)
                wide_hi(out, 1)

            out_phase("GO")
            ffn_in("FI0", 0, "FO0")
            out_phase("FO0")

            first_tiles("RI", 1, 0)
            n0, f0 = base["RI"], free0["RI"]

            def y_gelu(v, e):
                act.wait_ge(pair_free[e % 4], f0[e % 4] + e // 4 + 1)
                act.activation(gate(v), tmp[:, v % 3, :], ACT.Gelu_apprx_tanh).then_inc(y_act, 1)

            for u in range(2, 9):
                split_hi(n0 + u + 2)
            y_gelu(0, 8)
            act.wait_ge(hb_ready, 1)
            act.wait_ge(sp_ready, 1)
            for h in range(KD):
                e = 9 + h
                act.wait_ge(gates_done, h + 1)
                act.activation(halves(yt(h)), pair(e % 4), ACT.Tanh, scale=0.5, bias=hba[:, h:h + 1])\
                   .then_inc(pair_free[e % 4], 1)
            for h in range(KD):
                e = 9 + KD + h
                act.wait_ge(gates_done, KD + h + 1)
                act.wait_ge(tails, h + 1)
                act.activation(halves(xbt(h)), pair(e % 4), ACT.Tanh, scale=0.5, bias=hbx[:, h:h + 1])\
                   .then_inc(pair_free[e % 4], 1)
            for h in range(KD):
                act.wait_ge(p1_ready, h + 1)
                act.wait_ge(pair_free[(9 + h) % 4], f0[(9 + h) % 4] + (9 + h) // 4 + 1)
                act.activation(xc(h), yt(h), ACT.Tanh, scale=sp2[:, h:h + 1], bias=sp2[:, h:h + 1]).then_inc(t2_ready, 1)
                act.activation(yt(h), yt(h), ACT.Exp, scale=spm4[:, h:h + 1], bias=spm4[:, h:h + 1]).then_inc(a_ready, 1)
                if h % 4 == 3:
                    split_hi(n0 + 11 + h // 4)
            for h in range(KD):
                act.wait_ge(t2_ready, h + 1)
                act.activation(xc(h), xc(h), ACT.Sqrt, scale=0.25).then_inc(sqrt_ready, 1)
            for v in range(1, KD):
                if v == KD - 1:
                    wide_hi("RO", 0)
                    wide_hi("RO", 1)
                y_gelu(v, 24 + v)
                if v < KD - 2:
                    split_hi(n0 + 12 + v)

            out_phase("RO")
            ffn_in("FI1", 1, "FO1")
            out_phase("FO1")

            act.wait_ge(so_turned, 1)
            act.activation(wide[0:36, NT * D:(NT + 1) * D], psf[0:36, 4 * BANK:6 * BANK], ACT.Copy).then_inc(so_copied, 1)
            for b in range(2 * NT):
                if out_by_act(b):
                    act.wait_ge(out_turned, b + 1)
                    act.activation(out_tile(b), out_bank(b), ACT.Copy).then_inc(out_act, 1)

        @block.vector
        def _(dve):
            def split_lo(n, width=1024, i=0, per=0):
                s = slot(n)
                dve.wait_ge(hi_ready, i * per + (n + 1))
                dve.tensor_tensor(wlo[:, s, 0:width], stage[:, s, 0:width], whi[:, s, 0:width].bitcast(F32),
                                  ALU.subtract).then_inc(lo_ready, 1)

            def width_of(n):
                for name in ("FO0", "FO1"):
                    if base[name] <= n < base[name] + 24 and (n - base[name]) % 12 >= 10:
                        return 512
                return 1024

            def add_squares(q, r):
                if r == 0:
                    return
                if r >= 2:
                    dve.wait_ge(sq_added, 8 * q + r - 1)
                parts = [(0, TT)] if r < KD - 1 else [(0, HT), (HT, TT)]
                for j, (lo, hi) in enumerate(parts):
                    dve.wait_ge(sq_ready, 9 * q + r + j + 1)
                    dve.tensor_tensor(acc[:, lo:hi], acc[:, lo:hi], tmp[:, r % 3, lo:hi], ALU.add).then_inc(sq_added, 1)

            def diag_of(q):
                dve.wait_ge(std_ready, q + 1)
                dve.reciprocal(rtok[:, :], std[:, :]).then_inc(rtok_ready, 1)
                dve.wait_ge(rtok_ready, q + 1)
                dve.tensor_tensor(diag.rearrange("p (c t) -> p c t", c=NT),
                                  ident[:, :].unsqueeze(1).to_broadcast([P, NT, P]),
                                  bc3(rtok[:, :], P), ALU.mult).then_inc(diag_ready, 1)

            def h_low(k, q, layer, i):
                dve.wait_ge(h_hi, KD * (q // 2) + k + 1)
                dve.scalar_tensor_tensor(hl[:, k, :], xT[:, k, :], gain(layer, i, k), hh[:, k, :].bitcast(F32),
                                         ALU.mult, ALU.subtract).then_inc(h_lo, 1)

            def wide_lo(name, s):
                units = out_units(name)
                j = s % len(units)
                k, nk = units[j]
                at = 2 * (j % 4)
                src0 = (GATE0 if name == "RO" else 0) + k * TT
                dve.wait_ge(a_hi, AB[name] + s + 1)
                dve.tensor_tensor(hl[:, at:at + nk, :].rearrange("p k n -> p (k n)"), wide[:, src0:src0 + nk * TT],
                                  hh[:, at:at + nk, :].rearrange("p k n -> p (k n)").bitcast(F32),
                                  ALU.subtract).then_inc(a_lo, 1)

            dve.memset(acc[:, TT:NT * P], 0.0)
            dve.wait_ge(x_turned, 1)
            dve.tensor_copy(xT[:, :, T:TT], ps[:, 7, :].rearrange("p (k n) -> p k n", k=KD)).then_inc(x_ready, 1)

            def x_tile(k):
                dve.wait_ge(x_turned, k + 2)
                dve.tensor_copy(xT[:, k, 0:T], ps[:, 5 + k % 2, :]).then_inc(x_ready, 1)

            x_tile(0)
            dve.wait_ge(par1_ready, 1)
            for k in range(KD):
                if k + 1 < KD:
                    x_tile(k + 1)
                if k < 2:
                    split_lo(k, 2 * GW)
                h_low(k, 0, 0, 0)
                add_squares(0, k)
                if k in (2, 4):
                    split_lo(1 + k // 2, 2 * GW)
            diag_of(0)

            def v_evict(g, i=0):
                for t in range(NT):
                    if t < NC:
                        dve.wait_ge(v_tile_done, i * NC + (NC * g + t + 1))
                    else:
                        dve.wait_ge(unit_done, i * 4 + (4 * g + 4))
                    r = P if t < NC else TS
                    dve.scalar_tensor_tensor(z(i + g, t), ps[0:r, t, 0:GW], rtok[0:r, t:t + 1],
                                             brow[0:r, bass.ds(i * GW + g * GW, GW)], ALU.mult, ALU.add)\
                       .then_inc(z_evicted, 1)

            def v_stats(g, i=0):
                for t in range(NT):
                    r = P if t < NC else TS
                    dve.wait_ge(z_act, i * NT + (NT * g + t + 1))
                    dve.bn_stats(stats[0:r, t, bass.ds(i + g, 1), :].rearrange("p a s -> p (a s)"), z(i + g, t))\
                       .then_inc(z_stats, 1)

            def v_group(g, i=0, last=False):
                for j in range(4):
                    split_lo(4 * g + j + 2, 1024 if last and j >= 2 else 2 * GW, i, 0 if last or g < 3 else 4)
                    if j == 1:
                        v_stats(g - 1, i)
                v_evict(g, i)

            def softplus():
                lam = par[:, LAM0:LAM0 + KD]
                w = [spw[:, j, :] for j in range(5)]
                n = [0]

                def step(ins):
                    ins.then_inc(sp_chain, 1)
                    n[0] += 1
                    dve.wait_ge(sp_chain, n[0])

                dve.wait_ge(par2_ready, 1)
                step(dve.tensor_scalar(w[0], lam, -1.0, None, ALU.mult))
                step(dve.tensor_tensor(w[1], w[0], lam, ALU.max))
                dve.wait_ge(sp_exp, 1)
                step(dve.tensor_scalar(w[3], w[2], 2.0, None, ALU.add))
                step(dve.reciprocal(w[4], w[3]))
                step(dve.tensor_tensor(w[3], w[2], w[4], ALU.mult))
                step(dve.tensor_tensor(w[4], w[3], w[3], ALU.mult))
                step(dve.tensor_scalar(w[1], w[4], 2.0 / 19, None, ALU.mult))
                for odd in range(17, 1, -2):
                    step(dve.scalar_tensor_tensor(w[1], w[1], 2.0 / odd, w[4], ALU.add, ALU.mult))
                step(dve.scalar_tensor_tensor(w[1], w[1], 2.0, w[3], ALU.add, ALU.mult))
                step(dve.scalar_tensor_tensor(w[2], w[0], 0.0, w[1], ALU.max, ALU.add))
                dve.tensor_scalar(sp2[:, :], w[2], 2.0, None, ALU.mult)
                dve.tensor_scalar(spm4[:, :], w[2], -4.0, None, ALU.mult).then_inc(sp_ready, 1)
                dve.tensor_scalar(hba[:, :], par[:, BA0:BA0 + KD], 0.5, None, ALU.mult)
                dve.tensor_scalar(hbx[:, :], par[:, BX0:BX0 + KD], 0.5, None, ALU.mult).then_inc(hb_ready, 1)

            split_lo(4, 2 * GW)
            split_lo(5, 2 * GW)
            dve.wait_ge(brow_landed, 16)
            v_evict(0)
            v_group(1)
            v_group(2)
            softplus()
            with dve.Fori(0, GRP - 4) as i:
                v_group(3, i)
            v_group(GRP - 1, last=True)
            v_stats(GRP - 1)
            for t in range(NT):
                r = P if t < NC else TS
                dve.wait_ge(z_stats, NT * (GRP - 1) + t + 1)
                last = dve.bn_aggr(mv[0:r, t, :], stats[0:r, t, :, :].rearrange("p g s -> p (g s)"))
            last.then_inc(var_ready, 1)
            dve.wait_ge(lnstd_ready, 1)
            dve.reciprocal(lnr[:, 0:NC], lnr[:, 0:NC])
            dve.reciprocal(lnr[0:TS, NC:NT], lnr[0:TS, NC:NT]).then_inc(ln_ready, 1)
            dve.wait_ge(ln_ready, 1)

            def layer_norm(b, i, first=False):
                if not first:
                    dve.wait_ge(mix_done, i * (2 * FG) + (b - 1) * FG)
                    dve.wait_ge(v_stored[b], i * 16)
                dve.wait_ge(lnrow_landed[b], i * 32 + 32)
                for t in range(NT):
                    r = P if t < NC else TS
                    dve.scalar_tensor_tensor(vbuf[b][0:r, t, :], z(i * 2 + b, t), mv[0:r, t, 0:1],
                                             lnrow[b][0:r, 0:GW], ALU.subtract, ALU.mult).then_inc(ln_half, 1)
                for t in range(NT):
                    r = P if t < NC else TS
                    dve.wait_ge(ln_half, i * (2 * NT) + (b * NT + t + 1))
                    dve.scalar_tensor_tensor(vbuf[b][0:r, t, :], vbuf[b][0:r, t, :], lnr[0:r, t:t + 1],
                                             lnrow[b][0:r, GW:2 * GW], ALU.mult, ALU.add).then_inc(ln_done, 1)

            def mix_evict(x, xs, g):
                dve.wait_ge(mix_done, x + 1)
                bs = bsrow[:, bass.ds(g, 1), :]
                dve.tensor_tensor(wideA[:, bass.ds(xs * TT, T)].rearrange("p (c t) -> p c t", c=NC),
                                  ps[:, 6, :].rearrange("p (c t) -> p c t", c=NC),
                                  bs.to_broadcast([P, NC, P]), ALU.add)
                dve.tensor_tensor(wideA[:, bass.ds(xs * TT + T, TS)].rearrange("p (b t) -> p b t", b=NB),
                                  ps[:, 7, 0:TS].rearrange("p (b t) -> p b t", b=NB),
                                  bs[:, :, 0:NS].to_broadcast([P, NB, NS]), ALU.add).then_inc(pair_free[3], 1)

            def times_rb(out, m):
                return dve.tensor_tensor(halves(out), pair(m), halves(rb[:, :]), ALU.mult)

            def u_body(i, first=False, last=False):
                for c in range(6):
                    n = base["U"] + c
                    split_lo(n + 2, 1024, i, 6)
                    if c % 3 == 0:
                        layer_norm(c // 3, i, first)
                    if last and c == 5:
                        wide_lo("GO", 0)
                        wide_lo("GO", 1)
                    dve.wait_ge(unit_done, i * 6 + (n + 1))
                    if not (first and c < 3):
                        dve.wait_ge(gated, i * 6 + (c - 2))
                    times_rb(tmp[:, c % 3, :], c % 3).then_inc(pair_free[c % 3], 1)
                    if not (first and c < 2):
                        mix_evict(i * 6 + (c - 2), i * 6 + (c - 2), i * 2 + (c - 2) // 3)

            dve.wait_ge(rb_ready, 1)
            dve.wait_ge(bs_landed, 16)
            u_body(0, first=True)
            with dve.Fori(1, GRP // 2 - 1) as i:
                u_body(i)
            u_body(GRP // 2 - 1, last=True)
            for x in (DG // P - 2, DG // P - 1):
                mix_evict(x, x, x // FG)

            def out_phase(name):
                per, q = len(out_units(name)), NORM[name]
                for s in range(2 * per):
                    n = base[name] + s
                    if n + 2 < base["END"]:
                        split_lo(n + 2, width_of(n + 2))
                    if s + 2 < 2 * per:
                        wide_lo(name, s + 2)
                    if s % per == per - 1:
                        for m in range(4):
                            add_squares(q, 4 * (s // per) + m)
                diag_of(q)
                if base[name] + 2 * per < base["END"]:
                    split_lo(base[name] + 2 * per + 2)

            def normed(q, k, layer, i, last=False):
                if k < 2:
                    dve.wait_ge(rb_ready if k else bc_done, q + 1)
                dve.scalar_tensor_tensor(yt(k), yt(k), gain(layer, i, k), rb[:, :] if k else BC, ALU.mult, ALU.mult)\
                   .then_inc(t_ready, 1)
                if k == 0 or last and k % 2 == 0:
                    dve.wait_ge(t_ready, KD * (q // 2) + k + 1)
                    dve.tensor_tensor(xT[:, k, :], xT[:, k, :], yt(k), ALU.add).then_inc(x_last[0] if last else x0_ready, 1)

            def first_tiles(name, post, layer, i):
                q, n = NORM[name], base[name]
                normed(q - 1, 0, *post)
                for k in range(KD):
                    if k + 1 < KD:
                        normed(q - 1, k + 1, *post)
                    h_low(k, q, layer, i)
                    add_squares(q, k)
                diag_of(q)
                split_lo(n + 3)
                dve.wait_ge(rb_ready, q + 1)

            def ffn_evict(name, i, c, gated0, first=False):
                n = base[name] + c
                dve.wait_ge(unit_done, i * 4 + (n + 1))
                if c < 2:
                    times_rb(wtile(i * 2 + c), c).then_inc(pair_free[c], 1)
                else:
                    if not first:
                        dve.wait_ge(ffn_gated, i * 2 + (gated0 + c - 3))
                    times_rb(tmp[:, c - 2, :], c).then_inc(pair_free[c], 1)

            def ffn_in(name, post, layer, out):
                first_tiles(name, post, layer, 2)
                n, nb, g0 = base[name], KF // 2, KF * layer
                for c in range(4):
                    if c >= 2:
                        split_lo(n + c + 2)
                    ffn_evict(name, 0, c, g0, first=True)
                with dve.Fori(1, nb - 1) as i:
                    for c in range(4):
                        split_lo(n + c + 2, 1024, i, 4)
                        ffn_evict(name, i, c, g0)
                for c in range(4):
                    split_lo(n + 4 * (nb - 1) + c + 2)
                    if c == 3:
                        wide_lo(out, 0)
                        wide_lo(out, 1)
                    ffn_evict(name, nb - 1, c, g0)

            out_phase("GO")
            ffn_in("FI0", (0, 1), 0, "FO0")
            out_phase("FO0")

            first_tiles("RI", (0, 3), 1, 0)
            n0, f0 = base["RI"], free0["RI"]

            def conv(u):
                dve.wait_ge(tap0, u + 1)
                xs = xc(u)[:, T:TT].rearrange("p (b t) -> p b t", b=NB)
                for w in range(1, CW):
                    tap = par[:, CVW0 + w * KD + u:CVW0 + w * KD + u + 1]
                    if w > 1:
                        dve.wait_ge(tap_chain, 5 * u + 2 * w - 3)
                    dve.scalar_tensor_tensor(xc(u)[:, 0:T], xb_p(u, w), tap, xc(u)[:, 0:T], ALU.mult, ALU.add)\
                       .then_inc(tap_chain, 1)
                    if w > 1:
                        dve.wait_ge(tap_chain, 5 * u + 2 * w - 2)
                    dve.scalar_tensor_tensor(xs, xb_s(u)[:, :, w:w + NS], tap, xs, ALU.mult, ALU.add)\
                       .then_inc(tap_chain if w < CW - 1 else conv_done, 1)

            def head(h):
                dve.wait_ge(a_ready, h + 1)
                dve.wait_ge(p1s_ready, h + 1)
                dve.scalar_tensor_tensor(xbt(h), yt(h), 1.0, xbt(h), ALU.add, ALU.mult).then_inc(b_ready, 1)

            def scan(h):
                dve.wait_ge(seq_ready, h + 1)
                dve.tensor_tensor_scan(xc(h), yt(h), xbt(h), 0.0, ALU.mult, ALU.add).then_inc(scanned, 1)

            def y_evict(v, e):
                dve.wait_ge(unit_done, n0 + 8 + v + 1)
                if v >= 3:
                    dve.wait_ge(y_act, v - 2)
                times_rb(tmp[:, v % 3, :], e % 4).then_inc(pair_free[e % 4], 1)

            dve.wait_ge(pads_ready, 1)
            for u in range(KD):
                if u >= 2:
                    split_lo(n0 + u + 2)
                if u:
                    conv(u - 1)
                dve.wait_ge(unit_done, n0 + u + 1)
                m, s0 = u % 4, T - HT
                dve.tensor_tensor(xb_p(u, CW - 1, HT), ps[:, 2 * m, 0:HT], rb[:, 0:HT], ALU.mult)
                dve.tensor_tensor(xb_p(u, CW - 1 + HT, s0), ps[:, 2 * m + 1, 0:s0], rb[:, HT:T], ALU.mult)
                dve.tensor_tensor(xb_s(u)[:, :, CW - 1:], ps[:, 2 * m + 1, s0:HT].rearrange("p (b t) -> p b t", b=NB),
                                  rb[:, T:TT].rearrange("p (b t) -> p b t", b=NB), ALU.mult).then_inc(pair_free[m], 1)
            split_lo(n0 + KD + 2)
            conv(KD - 1)
            y_evict(0, 8)
            for h in range(KD):
                e = 9 + KD + h
                dve.wait_ge(pair_free[e % 4], f0[e % 4] + e // 4 + 1)
                dve.scalar_tensor_tensor(xbt(h), xbt(h), 1.0, xc(h), ALU.add, ALU.mult).then_inc(p1_ready, 1)
            split_lo(n0 + 11)
            split_lo(n0 + 12)
            for v in range(1, KD):
                if v == KD - 1:
                    head(KD - 2)
                    wide_lo("RO", 0)
                    wide_lo("RO", 1)
                y_evict(v, 24 + v)
                if v < KD - 1:
                    head(v - 1)
                if v >= 2:
                    scan(v - 2)
                if v < KD - 2:
                    split_lo(n0 + 12 + v)
            head(KD - 1)
            scan(KD - 2)
            scan(KD - 1)

            out_phase("RO")
            ffn_in("FI1", (1, 1), 1, "FO1")
            out_phase("FO1")
            for k in range(KD):
                normed(NORM["FO1"], k, 1, 3, last=True)
            for b in range(2 * NT):
                if not out_by_act(b):
                    dve.wait_ge(out_turned, b + 1)
                    dve.tensor_copy(out_tile(b), out_bank(b)).then_inc(out_dve, 1)

        @block.gpsimd
        def _(pool):
            pool.memset(ident[:, :], 0.0).then_inc(consts, 1)
            pool.wait_ge(consts, 1)
            pool.affine_select(out=ident[:, :], in_=ident[:, :], compare_op=ALU.not_equal, fill=1.0,
                               base=0, pattern=[[-1, P]], channel_multiplier=1).then_inc(consts, 1)
            pool.memset(epsc[:, :], EPS)
            pool.memset(ones[:, :], 1.0).then_inc(consts, 1)
            pool.memset(wsblk[:, :, :], 0.0)
            pool.wait_ge(ws_landed, 16)
            pool.affine_select(out=wraw, in_=wraw, compare_op=ALU.is_ge, fill=0.0,
                               base=0, pattern=[[0, GRP], [-1, P]], channel_multiplier=1).then_inc(ws_masked, 1)

            def ln_rows(b, g):
                for j, v in enumerate((gm_ln_g, gm_ln_b)):
                    pool.dma_start(lnrow[b][:, j * GW:(j + 1) * GW],
                                   v[0, bass.ds(g * GW, GW)].partition_broadcast(P)).then_inc(lnrow_landed[b], 16)

            pool.wait_ge(ws_ready, 2)
            for b in range(NB):
                pool.dma_start(wsblk[NS * b:NS * (b + 1), :, NS * b:NS * (b + 1)], wsT[0:NS, :, 0:NS])\
                    .then_inc(blk_landed, 16)
            ln_rows(0, 0)
            ln_rows(1, 1)

            def gate_u(x, i):
                pool.wait_ge(u_act, i * 6 + (x + 1))
                pool.wait_ge(pair_free[3], i * 6 + (x + 1))
                w = wtile(i * 6 + x)
                pool.tensor_tensor(w, w, tmp[:, x % 3, :], ALU.mult).then_inc(gated, 1)

            def u_body(i, last=False):
                for c in range(6):
                    if c % 3 == 0:
                        b = c // 3
                        pool.wait_ge(ln_done, i * (2 * NT) + (b + 1) * NT)
                        pool.dma_start(s_v[0].rearrange("b t e -> (b t) e")[:, bass.ds(i * (2 * GW) + b * GW, GW)],
                                       vbuf[b][0:TS, NC, :]).then_inc(v_stored[b], 16)
                        if not last:
                            ln_rows(b, i * 2 + (b + 2))
                    gate_u(c, i)

            with pool.Fori(0, GRP // 2 - 1) as i:
                u_body(i)
            u_body(GRP // 2 - 1, last=True)

            def residual(n):
                for k in range(1, KD):
                    pool.wait_ge(t_ready, KD * n + k + 1)
                    pool.tensor_tensor(xT[:, k, :], xT[:, k, :], yt(k), ALU.add).then_inc(res_ready, 1)

            def ffn_gate(name, layer):
                with pool.Fori(0, KF // 2) as i:
                    for c in range(2):
                        pool.wait_ge(f_act, i * 2 + (KF * layer + c + 1))
                        pool.wait_ge(pair_free[2 + c], i + (free0[name][2 + c] + 1))
                        w = wtile(i * 2 + c)
                        pool.tensor_tensor(w, w, tmp[:, c, :], ALU.mult).then_inc(ffn_gated, 1)

            residual(0)
            ffn_gate("FI0", 0)
            pool.wait_ge(a_lo, AB["RO"])
            pool.wait_ge(par2_ready, 1)
            xall = wide[:, 0:KD * XB].rearrange("p (h n) -> p h n", h=KD)
            pool.memset(xall[:, :, 0:CW - 1], 0.0)
            for h in range(KD):
                last = pool.tensor_copy(xb_s(h)[:, :, 0:CW - 1],
                                        hist[:, h, 0:NB * (CW - 1)].rearrange("p (b w) -> p b w", b=NB))
            last.then_inc(pads_ready, 1)
            residual(1)
            f0 = free0["RI"]
            for u in range(KD):
                pool.wait_ge(pair_free[u % 4], f0[u % 4] + u // 4 + 1)
                tap, cb = par[:, CVW0 + u:CVW0 + u + 1], par[:, CVB0 + u:CVB0 + u + 1]
                pool.tensor_scalar(xc(u)[:, 0:T], xb_p(u, 0), tap, cb, ALU.mult, ALU.add)
                pool.tensor_scalar(xc(u)[:, T:TT].rearrange("p (b t) -> p b t", b=NB), xb_s(u)[:, :, 0:NS],
                                   tap, cb, ALU.mult, ALU.add).then_inc(tap0, 1)
                pool.tensor_copy(sout[:, u, 0:3], xb_p(u, T, CW - 1))
                pool.tensor_copy(sout[:, u, 3:27].rearrange("p (b w) -> p b w", b=NB), xb_s(u)[:, :, NS:])\
                    .then_inc(tails, 1)

            def with_root(h):
                pool.wait_ge(sqrt_ready, h + 1)
                pool.tensor_tensor(xbt(h), xbt(h), xc(h), ALU.mult).then_inc(p1s_ready, 1)

            def gate_h(h):
                pool.wait_ge(scanned, h + 1)
                pool.wait_ge(y_act, h + 1)
                pool.tensor_copy(sout[:, h, 27:28], xc(h)[:, T - 1:T])
                pool.tensor_copy(sout[:, h, 28:36], xc(h)[:, T:TT].rearrange("p (b t) -> p b t", b=NB)[:, :, NS - 1])
                pool.tensor_tensor(gate(h), gate(h), xc(h), ALU.mult).then_inc(rg_gated, 1)

            with_root(0)
            with_root(1)
            for h in range(KD):
                pool.wait_ge(b_ready, h + 1)
                a0 = yt(h)[:, T:TT].rearrange("p (b t) -> p b t", b=NB)[:, :, 0]
                b0 = xbt(h)[:, T:TT].rearrange("p (b t) -> p b t", b=NB)[:, :, 0]
                pool.tensor_tensor(s8[:, h % 2, :], a0, hist[:, h, 24:32], ALU.mult).then_inc(pool_chain, 1)
                pool.wait_ge(pool_chain, 2 * h + 1)
                pool.tensor_tensor(b0, b0, s8[:, h % 2, :], ALU.add).then_inc(pool_chain, 1)
                pool.wait_ge(pool_chain, 2 * h + 2)
                pool.memset(a0, 0.0).then_inc(seq_ready, 1)
                if h + 2 < KD:
                    with_root(h + 2)
                if h:
                    gate_h(h - 1)
            gate_h(KD - 1)
            residual(2)
            ffn_gate("FI1", 1)
            for k in range(1, KD, 2):
                pool.wait_ge(t_ready, KD * 3 + k + 1)
                pool.tensor_tensor(xT[:, k, :], xT[:, k, :], yt(k), ALU.add).then_inc(x_last[1], 1)


_INS = ["x_prompt", "x_sample", "state_conv", "state_h", "norm_gains",
        "gm_w_in", "gm_b_in", "gm_ln_g", "gm_ln_b", "gm_w_s", "gm_b_s", "gm_w_out",
        "rg_w_in", "rg_conv_w", "rg_conv_b", "rg_w_a", "rg_b_a", "rg_w_x", "rg_b_x", "rg_lambda", "rg_w_out",
        "ffn_w_in", "ffn_w_out"]


def kernel(**inputs):
    import numpy as _np
    import concourse.bacc as _bacc
    from concourse import mybir as _mybir
    from concourse.bass_utils import run_bass_kernel_spmd as _run

    shape = {n: tuple(inputs[n].shape) for n in _INS}
    B, T, D = shape["x_prompt"]
    NBS, TSS, _ = shape["x_sample"]
    L, _, W, _ = shape["state_conv"]
    outs = [(B, T, D), (NBS, TSS, D), (L, B, W, D), (L, B, D), (L, NBS, W, D), (L, NBS, D),
            (shape["gm_ln_g"][0], NBS, TSS, shape["gm_ln_g"][1])]
    nc = _bacc.Bacc("TRN2", target_bir_lowering=False, num_devices=1, dynamic_dma_scratch_size=4096)
    arrays, args = {}, []
    for name in _INS:
        a = _np.ascontiguousarray(inputs[name])
        arrays[f"in_{name}_dram"] = a
        args.append(nc.dram_tensor(f"in_{name}_dram", a.shape, _mybir.dt.from_np(a.dtype), kind="ExternalInput").ap())
    for i, s in enumerate(outs):
        args.append(nc.dram_tensor(f"out_{i}_dram", s, _mybir.dt.float32, kind="ExternalOutput").ap())
    trunk_kernel(nc, *args)
    r = _run(nc, [arrays], core_ids=[0])
    return tuple(r.results[0][f"out_{i}_dram"] for i in range(len(outs)))
```

```python
from contextlib import ExitStack

import concourse.bass as bass
from concourse import mybir


F32 = mybir.dt.float32
F32R = mybir.dt.float32r
ALU = mybir.AluOpType
ACT = mybir.ActivationFunctionType

P = 128
EPS = 1e-6
BANK = 512


def plan(D, DG, DFF):
    counts = [("V", DG // 384 * 4), ("U", DG // P), ("GO", 2 * (DG // 256)), ("FI0", 2 * DFF // P),
              ("FO0", 2 * 12), ("RI", 2 * D // P), ("RO", 2 * (D // 256)), ("FI1", 2 * DFF // P),
              ("FO1", 2 * 12)]
    base, slots = {}, []
    for name, n in counts:
        base[name] = len(slots)
        for j in range(n):
            slots.append(j % 3 if name == "U" else len(slots) % 4)
    base["END"] = len(slots)
    return base, slots


def trunk_kernel(nc, x_prompt, x_sample, state_conv, state_h, norm_gains,
                 gm_w_in, gm_b_in, gm_ln_g, gm_ln_b, gm_w_s, gm_b_s, gm_w_out,
                 rg_w_in, rg_conv_w, rg_conv_b, rg_w_a, rg_b_a, rg_w_x, rg_b_x, rg_lambda, rg_w_out,
                 ffn_w_in, ffn_w_out,
                 y_prompt, y_sample, p_conv, p_h, s_conv, s_h, s_v):
    _, T, D = x_prompt.shape
    NB, NS, _ = x_sample.shape
    TS = NB * NS
    TT = T + TS
    HT = TT // 2
    KD = D // P
    DG = gm_w_out.shape[1]
    DFF = ffn_w_out.shape[1]
    GRP = gm_w_s.shape[1]
    GW = DG // GRP
    FG = GW // P
    KF = DFF // P
    CW = rg_conv_w.shape[1]
    NC = T // P
    NT = NC + 1
    assert TS == 64 and D == 1024 and GW == 384 and KF == 22 and CW == 4

    base, slot_of = plan(D, DG, DFF)

    def slot(n):
        return slot_of[n]

    def slot_free(n):
        return n - 2 if base["U"] <= n < base["GO"] + 3 else n - 3

    def landings(n):
        return sum(s == slot_of[n] for s in slot_of[:n + 1])

    with ExitStack() as ctx:
        def sb(name, shape, dt=F32):
            return ctx.enter_context(nc.sbuf_tensor(name, shape, dt))

        def sem(name):
            return ctx.enter_context(nc.semaphore(name))

        xT = sb("xT", [P, KD, TT])
        hh = sb("hh", [P, KD, TT], F32R)
        hl = sb("hl", [P, KD, TT], F32R)
        GSLOT = FG * TT
        ZW = NT * GW
        wide = sb("wide", [P, GSLOT + GRP * ZW])
        yb = sb("yb", [P, KD * TT])
        stage = sb("stage", [P, 4, 1024])
        whi = sb("whi", [P, 4, 1024], F32R)
        wlo = sb("wlo", [P, 4, 1024], F32R)
        acc = sb("acc", [P, NT * P])
        tmp = sb("tmp", [P, 3, TT])
        rb = sb("rb", [P, TT])
        par = sb("par", [P, 152])
        hist = sb("hist", [P, KD, 32])
        ident = sb("ident", [P, P])
        ones = sb("ones", [P, P])
        wsT = sb("wsT", [P, GRP, P])
        wsblk = sb("wsblk", [TS, GRP, TS])
        bsrow = sb("bsrow", [P, GRP, P])
        lnrow1 = sb("lnrow1", [P, 2 * GW])
        stats = sb("stats", [P, NT, GRP, 6])
        mv = sb("mv", [P, NT, 2])
        lnr = sb("lnr", [P, NT])
        std = sb("std", [P, NT])
        rtok = sb("rtok", [P, NT])
        pstd = sb("pstd", [P, 2, 3])
        prtok = sb("prtok", [P, 2, 3])
        epsc = sb("epsc", [P, 1])
        std_early = sb("std_early", [P, 1])
        sout = sb("sout", [P, KD, 36])
        hba = sb("hba", [P, KD])
        hbx = sb("hbx", [P, KD])
        sp2 = sb("sp2", [P, KD])
        spm4 = sb("spm4", [P, KD])
        spw = sb("spw", [P, 5, KD])
        s8 = sb("s8", [P, 2, NB])
        ps = ctx.enter_context(nc.psum_tensor("ps", [P, 8, BANK], F32))

        wideA = wide[:, :]
        psf = ps[:, :, :].rearrange("p b n -> p (b n)")

        def TOK(j):
            return ps[:, 0, BANK - NT:BANK] if j else ps[:, 7, HT:HT + NT]

        def BC(j, c):
            if j == 0:
                return psf[:, 6 * BANK + c * P:6 * BANK + min((c + 1) * P, TT)]
            return ps[:, c, HT:HT + P] if c < NC else ps[:, 0, HT + P:HT + P + TS]

        CH = HT // 3

        def half(h):
            return slice(h * HT, (h + 1) * HT)

        def PTOK(h):
            return ps[0:CH, h, HT:HT + 3]

        def PBC(h):
            return ps[:, 2 + h, 0:HT]

        def pdiag(h):
            return tmp[0:CH, 0, half(h)]

        diag = tmp[:, :, :].rearrange("p a n -> p (a n)")[:, 0:NT * P]

        def bc3(ap2, n):
            return ap2.unsqueeze(2).to_broadcast([ap2.shape[0], ap2.shape[1], n])

        def halves(ap2):
            return ap2.rearrange("p (h n) -> p h n", h=2)

        def pair(m, lo=0, hi=HT):
            return ps[:, 2 * m:2 * m + 2, lo:hi]

        def wtile(k):
            return wideA[:, bass.ds(k * TT, TT)]

        def yt(k):
            return yb[:, bass.ds(k * TT, TT)]

        def z(g, t):
            rows = P if t < NC else TS
            return wide[0:rows, bass.ds(g * ZW + (GSLOT + t * GW), GW)]

        xin = [wide[0:(P if c < NC else TS), c * D:(c + 1) * D] for c in range(NT)]
        RAW0 = GSLOT + GRP * ZW - 2 * P - D
        praw1 = wide[0:88, RAW0:RAW0 + P]
        praw2 = wide[0:64, RAW0 + P:RAW0 + 2 * P]
        sraw = wide[0:32, RAW0 + 2 * P:RAW0 + 2 * P + D]
        brow = yb[:, 0:DG]
        wraw = yb[:, DG:DG + GRP * P].rearrange("p (g s) -> p g s", g=GRP)
        vbuf = [yb[:, ZW * b:ZW * (b + 1)].rearrange("p (t e) -> p t e", t=NT) for b in range(2)]
        vlow = wide[0:TS, 0:GW]
        xs_hl = whi[:, :, 2 * GW:1024].rearrange("p j (k n) -> p j k n", k=2)
        lnrow = [yb[:, 2 * ZW:2 * ZW + 2 * GW], lnrow1[:, :]]
        XB = T + CW - 1 + NB * (NS + CW - 1)
        XBP = T + CW - 1
        XC0 = KD * XB
        GATE0 = XC0 + KD * TT
        WG0 = GATE0 + KD * TT
        assert WG0 + 2 * KD * P <= GSLOT + GRP * ZW

        def xb_p(h, k, n=T):
            return wide[:, h * XB + k:h * XB + k + n]

        def xb_s(h):
            return wide[:, h * XB + XBP:(h + 1) * XB].rearrange("p (b t) -> p b t", b=NB)

        def xbt(h):
            return wide[:, h * XB:h * XB + TT]

        def xc(h):
            return wide[:, XC0 + h * TT:XC0 + (h + 1) * TT]

        def gate(h):
            return wide[:, GATE0 + h * TT:GATE0 + (h + 1) * TT]

        def wg(mat, h):
            return wide[:, WG0 + (mat * KD + h) * P:WG0 + (mat * KD + h + 1) * P]

        def gain(layer, i, k):
            c = (layer * 4 + i) * KD + k
            return par[:, c:c + 1]

        BIN0, CVW0, CVB0, BA0, BX0, LAM0 = 64, 88, 120, 128, 136, 144

        landed = [sem(f"weights_landed{s}") for s in range(4)]
        hi_ready = sem("weights_hi_ready")
        lo_ready = sem("weights_lo_ready")
        unit_done = sem("unit_done")
        pair_free = [sem(f"pair_free{m}") for m in range(4)]
        h_pair_used = sem("h_pair_used")
        a_hi = sem("wide_hi_ready")
        a_lo = sem("wide_lo_ready")
        h_hi = sem("h_hi_ready")
        h_lo = sem("h_lo_ready")
        par1_landed = sem("par1_landed")
        par2_landed = sem("par2_landed")
        x_landed = [sem("x_landed_first"), sem("x_landed_second")]
        xs_landed = sem("x_sample_landed")
        ws_landed = sem("ws_landed")
        brow_landed = sem("brow_landed")
        bs_landed = sem("bs_landed")
        lnrow_landed = [sem("lnrow_landed0"), sem("lnrow_landed1")]
        v_stored = [sem("v_stored0"), sem("v_stored1")]
        wg_landed = sem("gate_weights_landed")
        blk_landed = sem("wsblk_landed")
        consts = sem("consts_ready")
        par1_turned, par1_ready = sem("par1_turned"), sem("par1_ready")
        par2_turned, par2_ready = sem("par2_turned"), sem("par2_ready")
        x_turned, x_ready = sem("x_turned"), sem("x_ready")
        ws_masked, ws_turned, ws_ready = sem("ws_masked"), sem("ws_turned"), sem("ws_ready")
        sq_ready, sq_added = sem("squares_ready"), sem("squares_added")
        tok_done, std_ready, diag_ready = sem("tok_done"), sem("std_ready"), sem("diag_ready")
        rtok_ready = sem("rtok_ready")
        bc_done, rb_ready = sem("bc_done"), sem("rb_ready")
        v_tile_done, z_evicted, z_act = sem("v_tile_done"), sem("z_evicted"), sem("z_activated")
        psq_ready, psq_added = sem("post_squares_ready"), sem("post_squares_added")
        ptok_done, pstd_ready, prtok_ready = sem("post_tok_done"), sem("post_std_ready"), sem("post_rtok_ready")
        pdiag_ready, pbc_done, prb_ready = sem("post_diag_ready"), sem("post_bc_done"), sem("post_rb_ready")
        z_stats, var_ready, lnstd_ready, ln_ready = sem("z_stats"), sem("var_ready"), sem("lnstd_ready"), sem("lnr_ready")
        ln_half, ln_done = sem("ln_half"), sem("ln_done")
        xs_ready, vlow_out, vlow_added = sem("xs_hl_ready"), sem("vlow_out"), sem("vlow_added")
        mix_done = sem("mix_done")
        u_act = sem("u_activated")
        gated = sem("gated")
        y_tile_done = sem("y_tile_done")
        t_ready, x0_ready, res_ready = sem("t_ready"), sem("residual0_ready"), sem("residual_ready")
        f_act = sem("g_activated")
        ffn_gated = sem("ffn_gated")
        sp_chain, sp_exp, sp_ready = sem("sp_chain"), sem("sp_exp"), sem("sp_ready")
        hb_ready = sem("half_bias_ready")
        pads_ready = sem("pads_ready")
        tap0, tap_chain, conv_done, tails = sem("tap0"), sem("tap_chain"), sem("conv_done"), sem("tails_saved")
        t2_ready, p1_ready = sem("t2_ready"), sem("p1_ready")
        a_ready, sqrt_ready = sem("a_ready"), sem("sqrt_ready")
        rooted, rooted_by_pool = sem("rooted"), sem("rooted_by_pool")
        b_ready, seq_ready = sem("b_ready"), sem("sequences_ready")
        pool_chain = sem("pool_chain")
        scanned, rg_gated = sem("scanned"), sem("rg_gated")
        y_act = sem("y_activated")
        gates_done = sem("gates_done")
        x_last = [sem("x_last_by_dve"), sem("x_last_by_pool")]
        out_turned, out_stored = sem("out_turned"), sem("out_stored")
        out_act, out_dve = sem("out_copied_by_act"), sem("out_copied_by_dve")
        so_turned, so_copied = sem("so_turned"), sem("so_copied")

        free0 = {}
        count = [0, 0, 0, 0]
        for name, add in (("U", (GRP, GRP, GRP, DG // P)), ("GO", (2,) * 4), ("FI0", (KF // 2,) * 4),
                          ("FO0", (2,) * 4), ("RI", (8,) * 4), ("RO", (2,) * 4), ("FI1", (KF // 2,) * 4),
                          ("FO1", (2,) * 4)):
            free0[name] = list(count)
            count = [a + b for a, b in zip(count, add)]
        free0["END"] = list(count)

        PRE = {"V": 0, "FI0": 1, "RI": 2, "FI1": 3}
        POST = {"GO": 0, "FO0": 1, "RO": 2, "FO1": 3}

        def count_post(p, h):
            return 2 * p + h + 1

        def count_sq(p, G, h, m):
            return 16 * p + 8 * G + 4 * h + m + 1

        def count_add(p, G, h, m):
            return 14 * p + (3 * h + m if G == 0 else 7 + 4 * h + m)

        def count_t(p, h, k):
            return 2 * KD * p + KD * h + k + 1

        def count_res(p, h, k):
            return count_t(p, h, k) - 1 - p

        def count_h(name, h, k):
            return KD + 2 * KD * (PRE[name] - 1) + KD * h + k + 1

        NEXT = {"GO": "FI0", "FO0": "RI", "RO": "FI1", "FO1": None}
        PRE_GAIN = {"FI0": (0, 2), "RI": (1, 0), "FI1": (1, 2)}
        POST_GAIN = [(0, 1), (0, 3), (1, 1), (1, 3)]
        JOIN = 5
        AB = {"GO": 0, "FO0": 24, "RO": 48, "FO1": 56}
        KO = {"GO": DG // P, "FO0": KF, "RO": KD, "FO1": KF}

        def out_units(name):
            k = KO[name]
            if k % 4 == 0:
                return [(j, 2) for j in range(0, k, 2)]
            return [(0, 1), (1, 1)] + [(j, 2) for j in range(2, k, 2)]

        PIECES = [(0, 0), (0, 1), (1, 0), (1, 1), (0, 2), (0, 3), (0, 4), (1, 2), (1, 3), (1, 4)]
        OUT_BANK = [6, 7, 4, 5, 0, 1, 2, 3, 6, 7]

        def x_by_dve(k):
            return k % 4 == 0

        def x_made(h, k):
            of = [x_by_dve(j) == x_by_dve(k) for j in range(KD)]
            return h * sum(of) + sum(of[:k + 1])

        def out_by_act(b):
            return b != 8

        def out_tile(b):
            hf, c = PIECES[b]
            return xin[c][:, hf * 4 * P:(hf + 1) * 4 * P]

        def out_bank(b):
            return ps[0:P if PIECES[b][1] < NC else TS, OUT_BANK[b], :]

        block = ctx.enter_context(nc.Block())

        @block.sync
        def _(sp):
            def load(n, src, width, shape, i=0, per=0):
                dst = stage[:, slot(n), 0:width].rearrange("p (k c) -> p k c", c=shape)
                if n >= 4:
                    sp.wait_ge(lo_ready, i * per + slot_free(n))
                sp.dma_start(dst, src).then_inc(landed[slot(n)], 16)

            def rows(w, r0, nk, c0, width):
                return w[r0:r0 + nk * P, bass.ds(c0, width)].rearrange("(k p) c -> p k c", p=P)

            sp.dma_start(praw1[0:64], norm_gains.rearrange("l i (k p) -> (l i k) p", p=P)).then_inc(par1_landed, 16)
            sp.dma_start(praw1[64:88], gm_b_in[0, 0:DG].rearrange("(k p) -> k p", p=P)).then_inc(par1_landed, 16)
            sp.dma_start(xin[NC], x_sample.rearrange("b t d -> (b t) d")).then_inc(xs_landed, 16)
            wv = gm_w_in[0]
            for b in range(2):
                sp.dma_start(wide[:, 0:NC * D].rearrange("p (c d) -> p c d", c=NC)[:, :, b * D // 2:(b + 1) * D // 2],
                             x_prompt[0].rearrange("(c p) d -> p c d", p=P)[:, :, b * D // 2:(b + 1) * D // 2])\
                  .then_inc(x_landed[b], 16)
                for n in (2 * b, 2 * b + 1):
                    load(n, rows(wv, 2 * P * n, 2, DG, GW), 2 * GW, GW)
            sp.dma_start(brow, gm_b_in[0, DG:2 * DG].partition_broadcast(P)).then_inc(brow_landed, 16)
            for j, (v, r) in enumerate(((rg_conv_w[0], 32), (rg_conv_b, 8), (rg_b_a[0], 8), (rg_b_x[0], 8), (rg_lambda, 8))):
                at = (0, 32, 40, 48, 56)[j]
                src = v if j in (2, 3) else v.rearrange("w (k p) -> (w k) p", p=P)
                sp.dma_start(praw2[at:at + r], src).then_inc(par2_landed, 16)
            sp.dma_start(sraw[0:24], state_conv[0].rearrange("b w d -> (b w) d")).then_inc(par2_landed, 16)
            sp.dma_start(sraw[24:32], state_h[0]).then_inc(par2_landed, 16)
            sp.dma_start(wraw, gm_w_s[0].rearrange("g t s -> t g s")).then_inc(ws_landed, 16)
            sp.dma_start(bsrow[:, :, :], gm_b_s[0].partition_broadcast(P)).then_inc(bs_landed, 16)
            with sp.Fori(0, GRP - 1) as i:
                c0 = sp.snap(i * GW + (DG + GW))
                seen = [sp.snap(i * 4 + slot_free(4 + j)) for j in range(4)]
                for j in range(4):
                    sp.wait_ge(lo_ready, seen[j])
                    sp.dma_start(stage[:, slot(4 + j), 0:2 * GW].rearrange("p (k c) -> p k c", c=GW),
                                 rows(wv, 2 * P * j, 2, c0, GW)).then_inc(landed[slot(4 + j)], 16)

            def in_phase(first, w, col, iters, per):
                with sp.Fori(0, iters) as i:
                    cols = [sp.snap(col(i, c)) for c in range(per)]
                    seen = [sp.snap(i * per + slot_free(first + c)) for c in range(per)]
                    for c in range(per):
                        sp.wait_ge(lo_ready, seen[c])
                        sp.dma_start(stage[:, slot(first + c), :].rearrange("p (k c) -> p k c", c=P),
                                     rows(w, 0, KD, cols[c], P)).then_inc(landed[slot(first + c)], 16)

            def out_phase(name, w):
                units = out_units(name)
                first, per = base[name], len(units)
                with sp.Fori(0, 2) as i:
                    c0 = sp.snap(i * (4 * P))
                    seen = [sp.snap(i * per + slot_free(first + j)) for j in range(per)]
                    for j, (k, nk) in enumerate(units):
                        sp.wait_ge(lo_ready, seen[j])
                        sp.dma_start(stage[:, slot(first + j), 0:nk * 4 * P].rearrange("p (k c) -> p k c", c=4 * P),
                                     rows(w, k * P, nk, c0, 4 * P)).then_inc(landed[slot(first + j)], 16)

            def ffn_col(i, c):
                return i * (2 * P) + (c * P if c < 2 else DFF + (c - 2) * P)

            in_phase(base["U"], wv, lambda i, c: i * (6 * P) + c * P, GRP // 2, 6)
            out_phase("GO", gm_w_out[0])
            in_phase(base["FI0"], ffn_w_in[0], ffn_col, KF // 2, 4)
            out_phase("FO0", ffn_w_out[0])
            sp.wait_ge(a_lo, AB["RO"])
            for m, w in enumerate((rg_w_a, rg_w_x)):
                sp.dma_start(wide[:, WG0 + m * KD * P:WG0 + (m + 1) * KD * P].rearrange("p (h j) -> p h j", h=KD),
                             w[0].rearrange("h i j -> i h j")).then_inc(wg_landed, 16)
            in_phase(base["RI"], rg_w_in[0], lambda i, c: i * (4 * P) + (D + c * P), 2, 4)
            in_phase(base["RI"] + KD, rg_w_in[0], lambda i, c: i * (4 * P) + c * P, 2, 4)
            out_phase("RO", rg_w_out[0])
            in_phase(base["FI1"], ffn_w_in[1], ffn_col, KF // 2, 4)
            out_phase("FO1", ffn_w_out[1])
            sp.wait_ge(so_copied, 1)
            st = wide[0:36, NT * D:(NT + 1) * D]
            sp.dma_start(p_conv[0, 0], st[0:3]).then_inc(out_stored, 16)
            sp.dma_start(s_conv[0].rearrange("b w d -> (b w) d"), st[3:27]).then_inc(out_stored, 16)
            sp.dma_start(p_h[0], st[27:28]).then_inc(out_stored, 16)
            sp.dma_start(s_h[0], st[28:36]).then_inc(out_stored, 16)
            for b in range(2 * NT):
                hf, c = PIECES[b]
                on_act = out_by_act(b)
                sp.wait_ge(out_act if on_act else out_dve, sum(out_by_act(x) == on_act for x in range(b + 1)))
                dst = y_prompt[0, c * P:(c + 1) * P, :] if c < NC else y_sample.rearrange("b t d -> (b t) d")
                sp.dma_start(dst[:, hf * 4 * P:(hf + 1) * 4 * P], out_tile(b)).then_inc(out_stored, 16)
            sp.wait_ge(out_stored, 16 * (4 + 2 * NT))
            for b in range(2):
                sp.wait_ge(v_stored[b], 16 * (GRP // 2))

        @block.tensor
        def _(pe):
            def mm(out, w, x, start, stop):
                return pe.matmul(out, w, x, start=start, stop=stop)

            def three(m, hi_w, lo_w, k, first, last):
                a, b = ps[:, 2 * m, 0:HT], ps[:, 2 * m + 1, 0:HT]
                mm(a, hi_w, hh[:, k, 0:HT], first, False)
                mm(b, hi_w, hh[:, k, HT:TT], first, False)
                mm(a, hi_w, hl[:, k, 0:HT], False, False)
                mm(b, hi_w, hl[:, k, HT:TT], False, False)
                mm(a, lo_w, hh[:, k, 0:HT], False, last)
                return mm(b, lo_w, hh[:, k, HT:TT], False, last)

            def one_half(m, h, hi_w, lo_w, k, first, last):
                o = ps[:, 2 * m + h, 0:HT]
                mm(o, hi_w, hh[:, k, half(h)], first, False)
                mm(o, hi_w, hl[:, k, half(h)], False, False)
                return mm(o, lo_w, hh[:, k, half(h)], False, last)

            def token_sums(j):
                for c in range(NT):
                    if c in (0, 2):
                        pe.wait_ge(sq_added, 8 * j + (7 if c == 0 else 8))
                    last = mm(TOK(j)[:, c:c + 1], acc[:, c * P:(c + 1) * P], ones[:, 0:1], True, True)
                last.then_inc(tok_done, 1)

            def spread(j):
                pe.wait_ge(diag_ready, j + 1)
                for c in range(NT):
                    r = P if c < NC else TS
                    last = mm(BC(j, c), ones[0:r, :], diag[0:r, c * P:c * P + r], True, True)
                last.then_inc(bc_done, 1)

            def post_sums(p, h):
                pe.wait_ge(psq_added, count_add(p, 1, h, 3))
                for c in range(3):
                    at = h * HT + c * CH
                    last = mm(PTOK(h)[:, c:c + 1], acc[:, at:at + CH], ones[:, 0:1], True, True)
                last.then_inc(ptok_done, 1)

            def post_spread(p, h):
                pe.wait_ge(pdiag_ready, count_post(p, h))
                mm(PBC(h), ones[0:CH, :], pdiag(h), True, True).then_inc(pbc_done, 1)

            pe.wait_ge(consts, 3)
            pe.wait_ge(par1_landed, 32)
            pe.transpose(ps[:, 0, 0:88], praw1, ident[0:88, 0:88]).then_inc(par1_turned, 1)
            pe.wait_ge(xs_landed, 16)
            for k in range(KD):
                last = pe.transpose(ps[:, 7, k * TS:(k + 1) * TS], xin[NC][:, k * P:(k + 1) * P], ident[0:TS, 0:TS])
            last.then_inc(x_turned, 1)

            def turn_x(k):
                if k % 4 == 0:
                    pe.wait_ge(x_landed[k // 4], 16)
                if k >= 2:
                    pe.wait_ge(x_ready, k)
                for c in range(NC):
                    last = pe.transpose(ps[:, 5 + k % 2, c * P:(c + 1) * P], xin[c][:, k * P:(k + 1) * P], ident[:, :])
                last.then_inc(x_turned, 1)

            turn_x(0)
            turn_x(1)

            def v_group(g, first, i=0):
                for j in range(4):
                    n = 4 * g + j
                    pe.wait_ge(lo_ready, i * 4 + (n + 1))
                    for kk in range(2):
                        k = 2 * j + kk
                        if first:
                            if k + 2 < KD:
                                turn_x(k + 2)
                            pe.wait_ge(h_lo, k + 1)
                        wh = whi[:, slot(n), kk * GW:(kk + 1) * GW]
                        wl = wlo[:, slot(n), kk * GW:(kk + 1) * GW]
                        for t in range(NT):
                            if k == KD - 1 and first and t == 1:
                                token_sums(0)
                            if k == 0 and first and t == 0:
                                pe.wait_ge(par1_ready, 1)
                            if k == 0 and not first:
                                pe.wait_ge(z_evicted, i * NT + (NT * (g - 1) + t + 1))
                            r = P if t < NC else TS
                            o = ps[0:r, t, 0:GW]
                            c = slice(t * P, t * P + r)
                            if t < NC or first:
                                mm(o, hh[:, k, c], wh, k == 0, False)
                                mm(o, hl[:, k, c], wh, False, False)
                                last = mm(o, hh[:, k, c], wl, False, k == KD - 1)
                            else:
                                if k:
                                    mm(o, hh[:, k, c], wl, False, False)
                                last = mm(ps[:, t, 0:GW], xs_hl[:, j, kk, :], wh, k == 0, k == KD - 1)
                                if k == 0:
                                    last = mm(o, hh[:, k, c], wl, False, False)
                            if k == KD - 1 and t < NC:
                                last.then_inc(v_tile_done, 1)
                    last.then_inc(unit_done, 1)

            v_group(0, True)
            pe.wait_ge(xs_ready, 1)
            v_group(1, False)
            pe.wait_ge(ws_masked, 1)
            for g in range(GRP):
                at = 4 * BANK + BANK + g * P if g < 4 else 6 * BANK + g * P - 4 * P
                last = pe.transpose(psf[:, at:at + P], wraw[:, g, :], ident[:, :])
                if g == 3:
                    last.then_inc(ws_turned, 1)
            last.then_inc(ws_turned, 1)
            v_group(2, False)
            pe.wait_ge(ws_ready, 2)
            pe.wait_ge(par2_landed, 16 * 7)
            pe.transpose(ps[:, 5, 0:64], praw2, ident[0:64, 0:64])
            for k in range(KD):
                last = pe.transpose(ps[:, 5, 64 + 32 * k:96 + 32 * k], sraw[:, k * P:(k + 1) * P], ident[0:32, 0:32])
            last.then_inc(par2_turned, 1)
            spread(0)
            with pe.Fori(0, GRP - 3) as i:
                v_group(3, False, i)

            def mix(x, f, b, g):
                pe.wait_ge(pair_free[3], x)
                for c in range(NC):
                    mm(ps[:, 6, c * P:(c + 1) * P], vbuf[b][:, c, f * P:(f + 1) * P],
                       wsT[:, bass.ds(g, 1), :].rearrange("p a t -> p (a t)"), True, True)
                mm(ps[:, 7, 0:TS], vbuf[b][0:TS, NC, f * P:(f + 1) * P],
                   wsblk[:, bass.ds(g, 1), :].rearrange("p a t -> p (a t)"), True, True).then_inc(mix_done, 1)

            def u_body(i, first=False, last_body=False):
                for c in range(6):
                    n = base["U"] + c
                    m = c % 3
                    pe.wait_ge(lo_ready, i * 6 + (n + 1))
                    if first and c < 3:
                        pe.wait_ge(z_evicted, NT * (GRP - 1) + min(2 * c + 2, NT))
                    else:
                        pe.wait_ge(pair_free[m], i * 2 + (c // 3))
                    for k in range(KD):
                        if last_body and c == 5 and k in (2, 5):
                            mix(i * 6 + 3 + k // 5, k // 5, 1, i * 2 + 1)
                        at = three(m, whi[:, slot(n), k * P:(k + 1) * P], wlo[:, slot(n), k * P:(k + 1) * P],
                                   k, k == 0, k == KD - 1)
                        if last_body and c == 5 and k % 2 and k < KD - 1:
                            at.then_inc(h_pair_used, 1)
                    at.then_inc(unit_done, 1)
                    if first and c < 2 or last_body and c == 5:
                        continue
                    if c % 3 == 2:
                        pe.wait_ge(ln_done, i * (2 * NT) + (c // 3 + 1) * NT)
                    gshift, f = divmod(c - 2, 3)
                    if first and c == 2:
                        pe.wait_ge(blk_landed, 16 * NB)
                        pe.wait_ge(rb_ready, 1)
                    mix(i * 6 + (c - 2), f, gshift % 2, i * 2 + gshift)

            u_body(0, first=True)
            with pe.Fori(1, GRP // 2 - 1) as i:
                u_body(i)
            u_body(GRP // 2 - 1, last_body=True)
            mix(DG // P - 1, FG - 1, 1, GRP - 1)

            def out_phase(name):
                units = out_units(name)
                per, p = len(units), POST[name]

                def weights(n, kk, m):
                    at = kk * 4 * P + m * P
                    return whi[:, slot(n), at:at + P], wlo[:, slot(n), at:at + P]

                for G in range(2):
                    first = base[name] + G * per
                    for j in range(per - 2):
                        pe.wait_ge(lo_ready, first + j + 1)
                        pe.wait_ge(a_lo, G * per + AB[name] + j + 1)
                        for kk in range(units[j][1]):
                            for m in range(4):
                                if j == 0 and kk == 0:
                                    pe.wait_ge(pair_free[m], G + free0[name][m])
                                last = three(m, *weights(first + j, kk, m), 2 * (j % 4) + kk, j == 0 and kk == 0, False)
                        last.then_inc(unit_done, 1)
                    for h in range(2):
                        for j in (per - 2, per - 1):
                            if h == 0:
                                pe.wait_ge(lo_ready, first + j + 1)
                                pe.wait_ge(a_lo, G * per + AB[name] + j + 1)
                            for m in range(4):
                                for kk in range(2):
                                    last = one_half(m, h, *weights(first + j, kk, m), 2 * (j % 4) + kk, False,
                                                    (j, kk) == (per - 1, 1))
                                if h == 1 and m == 3:
                                    last.then_inc(unit_done, 1)
                                elif j == per - 1:
                                    last.then_inc(y_tile_done, 1)
                                if (G, h, j) == (1, 1, per - 2):
                                    if m == 1:
                                        post_sums(p, 0)
                                    if m == 3:
                                        post_spread(p, 0)

            def first_tiles(name):
                n, j, p = base[name], PRE[name], PRE[name] - 1

                def part(m, h, k):
                    return one_half(m, h, whi[:, slot(n + m), k * P:(k + 1) * P], wlo[:, slot(n + m), k * P:(k + 1) * P],
                                    k, k == 0, k == KD - 1)

                pe.wait_ge(h_hi, count_h(name, 0, 0))
                for m in range(3):
                    pe.wait_ge(lo_ready, n + m + 1)
                    pe.wait_ge(pair_free[m], free0[name][m])
                    for w in (whi, wlo):
                        mm(ps[:, 2 * m, 0:HT], w[:, slot(n + m), 0:P], hh[:, 0, half(0)], w is whi, False)
                pe.wait_ge(h_lo, count_h(name, 0, 0))
                for m in range(3):
                    mm(ps[:, 2 * m, 0:HT], whi[:, slot(n + m), 0:P], hl[:, 0, half(0)], False, False)
                for k in range(1, KD):
                    pe.wait_ge(h_lo, count_h(name, 0, k))
                    for m in range(3):
                        part(m, 0, k)
                    if k == 2:
                        post_sums(p, 1)
                    if k == JOIN:
                        pe.wait_ge(lo_ready, n + 4)
                        pe.wait_ge(pair_free[3], free0[name][3])
                        for before in range(k):
                            part(3, 0, before)
                    if k >= JOIN:
                        part(3, 0, k)
                    if k == 4:
                        post_spread(p, 1)
                for k in range(KD - 3):
                    pe.wait_ge(h_lo, count_h(name, 1, k))
                    for m in range(4):
                        part(m, 1, k)
                for m in range(4):
                    for k in range(KD - 3, KD):
                        if m == 0:
                            pe.wait_ge(h_lo, count_h(name, 1, k))
                        last = part(m, 1, k)
                    last.then_inc(unit_done, 1)
                    if m == 0:
                        token_sums(j)
                    if m == 2:
                        spread(j)

            def tile_unit(n, m, freed, last_unit, i=0, per=0):
                pe.wait_ge(lo_ready, i * per + (n + 1))
                pe.wait_ge(pair_free[m], freed)
                for k in range(KD):
                    last = three(m, whi[:, slot(n), k * P:(k + 1) * P], wlo[:, slot(n), k * P:(k + 1) * P],
                                 k, k == 0, k == KD - 1)
                    if last_unit and k % 2 and k < KD - 1:
                        last.then_inc(h_pair_used, 1)
                last.then_inc(unit_done, 1)

            def ffn_in(name):
                first_tiles(name)
                nb = KF // 2
                with pe.Fori(1, nb - 1) as i:
                    for c in range(4):
                        tile_unit(base[name] + c, c, i + free0[name][c], False, i, 4)
                for c in range(4):
                    tile_unit(base[name] + 4 * (nb - 1) + c, c, nb - 1 + free0[name][c], c == 3)

            out_phase("GO")
            ffn_in("FI0")
            out_phase("FO0")

            first_tiles("RI")
            f0 = free0["RI"]
            for u in range(4, 9):
                tile_unit(base["RI"] + u, u % 4, f0[u % 4] + u // 4, False)
            pe.wait_ge(wg_landed, 32)
            e = 9
            for mat in range(2):
                for h in range(KD):
                    if mat == 0:
                        pe.wait_ge(conv_done, h + 1)
                    pe.wait_ge(pair_free[e % 4], f0[e % 4] + e // 4)
                    for b in range(2):
                        last = mm(ps[:, 2 * (e % 4) + b, 0:HT], wg(mat, h), xc(h)[:, half(b)], True, True)
                    last.then_inc(gates_done, 1)
                    e += 1
            for u in range(9, 16):
                tile_unit(base["RI"] + u, e % 4, f0[e % 4] + e // 4, u == 15)
                e += 1

            out_phase("RO")
            ffn_in("FI1")
            out_phase("FO1")

            post_sums(POST["FO1"], 1)
            pe.wait_ge(pair_free[2], free0["END"][2])
            for k in range(KD):
                last = pe.transpose(ps[0:36, 4 + k // 4, (k % 4) * P:(k % 4 + 1) * P], sout[:, k, :], ident[:, :])
            last.then_inc(so_turned, 1)
            pe.wait_ge(pair_free[3], free0["END"][3])
            for h in range(2):
                for k in range(KD):
                    pe.wait_ge(x_last[0 if x_by_dve(k) else 1], x_made(h, k))
                    if (h, k) == (0, 2):
                        post_spread(POST["FO1"], 1)
                    if (h, k) == (0, 4):
                        pe.wait_ge(so_copied, 1)
                    if (h, k) == (1, 4):
                        pe.wait_ge(out_act, 2)
                    for b, (hf, c) in enumerate(PIECES):
                        if hf == k // 4 and (c >= 2) == (h == 1):
                            r = P if c < NC else TS
                            last = pe.transpose(out_bank(b)[:, (k % 4) * P:(k % 4 + 1) * P],
                                                xT[:, k, c * P:c * P + r], ident[:, :])
                            if k % 4 == 3:
                                last.then_inc(out_turned, 1)

        @block.scalar
        def _(act):
            def split_hi(n, width=1024, i=0, per=0):
                s = slot(n)
                turns = {0: 0, 4: 1, 6: 2}[per]
                act.wait_ge(landed[s], i * (16 * turns) + 16 * landings(n))
                if n >= 4:
                    act.wait_ge(unit_done, i * per + slot_free(n))
                act.activation(whi[:, s, 0:width], stage[:, s, 0:width], ACT.Copy).then_inc(hi_ready, 1)

            def width_of(n):
                for name in ("FO0", "FO1"):
                    if base[name] <= n < base[name] + 24 and (n - base[name]) % 12 < 2:
                        return 512
                return 1024

            def std_of(j):
                act.wait_ge(tok_done, j + 1)
                act.activation(std[:, :], TOK(j), ACT.Sqrt, scale=1.0 / D, bias=epsc[:, 0:1]).then_inc(std_ready, 1)

            def rb_of(j):
                act.wait_ge(bc_done, j + 1)
                if j == 0:
                    act.activation(rb[:, 0:T], ps[:, 6, :], ACT.Copy)
                else:
                    act.activation(rb[:, 0:T].rearrange("p (c n) -> p c n", c=NC), ps[:, 0:NC, HT:HT + P], ACT.Copy)
                act.activation(rb[:, T:TT], BC(j, NC), ACT.Copy).then_inc(rb_ready, 1)

            def post_std(p, h):
                act.wait_ge(ptok_done, count_post(p, h))
                act.activation(pstd[0:CH, h, :], PTOK(h), ACT.Sqrt, scale=1.0 / D, bias=epsc[0:CH, 0:1])\
                   .then_inc(pstd_ready, 1)

            def post_rb(p, h):
                act.wait_ge(pbc_done, count_post(p, h))
                if h == 0:
                    act.wait_ge(t_ready, count_t(p, 0, 0))
                act.activation(rb[:, half(h)], PBC(h), ACT.Copy).then_inc(prb_ready, 1)

            def square(j, r):
                if r >= 4:
                    act.wait_ge(sq_added, 8 * j + r - 3)
                dst = tmp[:, r % 3, :] if r else acc[:, 0:TT]
                for at in ([slice(0, TT)] if r < KD - 1 else [half(0), half(1)]):
                    act.activation(dst[:, at], xT[:, r, at], ACT.Square).then_inc(sq_ready, 1)

            def y_out(p, G, h, m):
                r, src = 4 * G + m, ps[:, 2 * m + h, 0:HT]
                if r >= 4:
                    act.wait_ge(psq_added, count_add(p, (r - 3) // 4, h, (r - 3) % 4))
                act.activation(tmp[:, r % 3, half(h)] if r else acc[:, half(h)], src, ACT.Square).then_inc(psq_ready, 1)
                copied = act.activation(yt(r)[:, half(h)], src, ACT.Copy)
                if h == 1:
                    copied.then_inc(pair_free[m], 1)

            def h_high(k, layer, i, at):
                act.activation(hh[:, k, at], xT[:, k, at], ACT.Copy, scale=gain(layer, i, k)).then_inc(h_hi, 1)

            def source(name, k, nk):
                if name == "RO":
                    return wide[:, GATE0 + k * TT:GATE0 + (k + nk) * TT]
                return wide[:, k * TT:(k + nk) * TT]

            def wide_hi(name, s):
                units = out_units(name)
                j = s % len(units)
                k, nk = units[j]
                act.wait_ge({"GO": gated, "RO": rg_gated}.get(name, ffn_gated),
                            k + nk + (KF if name == "FO1" else 0))
                if s < 3:
                    act.wait_ge(h_pair_used, 3 * POST[name] + s + 1)
                else:
                    act.wait_ge(unit_done, base[name] + max(s - 3, 0))
                at = 2 * (j % 4)
                act.activation(hh[:, at:at + nk, :].rearrange("p k n -> p (k n)"), source(name, k, nk),
                               ACT.Copy).then_inc(a_hi, 1)

            act.wait_ge(consts, 3)
            act.activation(std_early[:, :], epsc[:, :], ACT.Sqrt)
            act.wait_ge(par1_turned, 1)
            act.activation(par[:, 0:88], ps[:, 0, 0:88], ACT.Copy).then_inc(par1_ready, 1)
            split_hi(0, 2 * GW)
            split_hi(1, 2 * GW)
            act.wait_ge(par1_ready, 1)
            for k in range(KD):
                act.wait_ge(x_ready, k + 2)
                h_high(k, 0, 0, slice(0, TT))
                square(0, k)
                if k in (2, 4, 6):
                    split_hi(1 + k // 2, 2 * GW)
            split_hi(5, 2 * GW)
            act.wait_ge(h_lo, KD)
            for src, at in ((hh, 0), (hl, TS)):
                for kk in range(2):
                    last = act.activation(xs_hl[:, :, kk, at:at + TS], src[:, kk::2, T:TT], ACT.Copy)
            last.then_inc(xs_ready, 1)
            std_of(0)

            def v_gelu(g, i=0):
                for t in range(NT):
                    act.wait_ge(z_evicted, i * NT + (NT * g + t + 1))
                    zt = z(i + g, t)
                    act.activation(zt, zt, ACT.Gelu_apprx_tanh).then_inc(z_act, 1)

            def v_group(g, i=0, last=False):
                for j in range(4):
                    split_hi(4 * g + j + 2, 1024 if last and j >= 2 else 2 * GW, i, 0 if last or g < 3 else 4)
                act.wait_ge(unit_done, i * 4 + (4 * g + 4))
                if g > 1:
                    act.wait_ge(z_evicted, i * NT + NT * g)
                act.activation(vlow, ps[TS:2 * TS, NC, 0:GW], ACT.Copy).then_inc(vlow_out, 1)
                v_gelu(g, i)

            v_gelu(0)
            v_group(1)
            for b in range(2):
                act.wait_ge(ws_turned, b + 1)
                act.activation(wsT[:, 4 * b:4 * b + 4, :].rearrange("p g t -> p (g t)"),
                               ps[:, 5 + b, :], ACT.Copy).then_inc(ws_ready, 1)
            v_group(2)
            act.wait_ge(par2_turned, 1)
            act.activation(par[:, 88:152], ps[:, 5, 0:64], ACT.Copy)
            act.activation(hist[:, :, :].rearrange("p k c -> p (k c)"), ps[:, 5, 64:320], ACT.Copy).then_inc(par2_ready, 1)
            rb_of(0)
            act.wait_ge(sp_chain, 2)
            act.activation(spw[:, 2, :], spw[:, 1, :], ACT.Exp, scale=-1.0).then_inc(sp_exp, 1)
            with act.Fori(0, GRP - 4) as i:
                v_group(3, i)
            v_group(GRP - 1, last=True)
            act.wait_ge(var_ready, 1)
            act.activation(lnr[:, 0:NC], mv[:, 0:NC, 1], ACT.Sqrt, bias=epsc[:, 0:1])
            act.activation(lnr[0:TS, NC:NT], mv[0:TS, NC, 1:2], ACT.Sqrt, bias=epsc[0:TS, 0:1]).then_inc(lnstd_ready, 1)

            def u_body(i, last=False):
                for c in range(6):
                    m = c % 3
                    if last and c == 5:
                        wide_hi("GO", 0)
                        wide_hi("GO", 1)
                    split_hi(base["U"] + c + 3, 1024, i, 6)
                    act.wait_ge(pair_free[m], i * 2 + (c // 3 + 1))
                    act.activation(tmp[:, m, :], tmp[:, m, :], ACT.Gelu_apprx_tanh,
                                   bias=par[:, bass.ds(i * 6 + (BIN0 + c), 1)]).then_inc(u_act, 1)

            split_hi(base["U"] + 2)
            with act.Fori(0, GRP // 2 - 1) as i:
                u_body(i)
            u_body(GRP // 2 - 1, last=True)

            def out_phase(name):
                units = out_units(name)
                per, p = len(units), POST[name]
                act.activation(std_early[:, :], epsc[:, :], ACT.Sqrt)
                for s in range(2 * per):
                    n = base[name] + s
                    if n > base["GO"] and n + 2 < base["END"]:
                        split_hi(n + 2, width_of(n + 2))
                    if s + 2 < 2 * per:
                        wide_hi(name, s + 2)
                    if s % per == per - 1:
                        G = s // per
                        if name == "GO" and G == 0:
                            for b in range(2):
                                act.wait_ge(v_stored[b], 16 * (GRP // 2))
                        for h in range(2):
                            for m in range(4):
                                if (G, h, m) == (1, 1, 3):
                                    break
                                if (h, m) == (1, 3):
                                    act.wait_ge(unit_done, n + 1)
                                else:
                                    act.wait_ge(y_tile_done, 14 * p + 7 * G + 4 * h + m + 1)
                                y_out(p, G, h, m)
                                if (G, h, m) == (1, 0, 3):
                                    post_std(p, 0)
                                    if NEXT[name]:
                                        split_hi(n + 3)
                                    post_rb(p, 0)
                                    if NEXT[name]:
                                        high(NEXT[name], 0, 0)
                                if (G, h, m) == (1, 1, 1) and NEXT[name]:
                                    high(NEXT[name], 0, 1)

            def high(name, h, k):
                if (h, k) == (0, 0):
                    act.wait_ge(x0_ready, PRE[name])
                else:
                    act.wait_ge(res_ready, count_res(PRE[name] - 1, h, k))
                h_high(k, *PRE_GAIN[name], half(h))

            def first_tiles(name):
                j, p, n = PRE[name], PRE[name] - 1, base[name]
                high(name, 0, 2)
                act.wait_ge(unit_done, n)
                y_out(p, 1, 1, 3)
                high(name, 0, 3)
                post_std(p, 1)
                high(name, 0, 4)
                split_hi(n + 3)
                high(name, 0, 5)
                post_rb(p, 1)
                high(name, 0, 6)
                high(name, 0, 7)
                for k in range(KD):
                    high(name, 1, k)
                    square(j, k)
                std_of(j)
                split_hi(n + 4)
                rb_of(j)

            def silu(name, i, c):
                act.wait_ge(pair_free[c], i + (free0[name][c] + 1))
                w = wtile(i * 2 + c)
                act.activation(w, w, ACT.Silu).then_inc(f_act, 1)

            def ffn_in(name, out):
                first_tiles(name)
                n, nb = base[name], KF // 2
                silu(name, 0, 0)
                silu(name, 0, 1)
                split_hi(n + 5)
                with act.Fori(1, nb - 1) as i:
                    for c in range(4):
                        split_hi(n + c + 2, 1024, i, 4)
                        if c < 2:
                            silu(name, i, c)
                for c in range(4):
                    split_hi(n + 4 * (nb - 1) + c + 2)
                    if c < 2:
                        silu(name, nb - 1, c)
                wide_hi(out, 0)
                wide_hi(out, 1)

            out_phase("GO")
            ffn_in("FI0", "FO0")
            out_phase("FO0")

            first_tiles("RI")
            n0, f0 = base["RI"], free0["RI"]

            def y_gelu(v, e):
                act.wait_ge(pair_free[e % 4], f0[e % 4] + e // 4 + 1)
                act.activation(gate(v), tmp[:, v % 3, :], ACT.Gelu_apprx_tanh).then_inc(y_act, 1)

            for u in range(3, 9):
                split_hi(n0 + u + 2)
            y_gelu(0, 8)
            act.wait_ge(hb_ready, 1)
            act.wait_ge(sp_ready, 1)
            for h in range(KD):
                e = 9 + h
                act.wait_ge(gates_done, h + 1)
                act.activation(halves(yt(h)), pair(e % 4), ACT.Tanh, scale=0.5, bias=hba[:, h:h + 1])\
                   .then_inc(pair_free[e % 4], 1)
            for h in range(KD):
                e = 9 + KD + h
                act.wait_ge(gates_done, KD + h + 1)
                act.wait_ge(tails, h + 1)
                act.activation(halves(xbt(h)), pair(e % 4), ACT.Tanh, scale=0.5, bias=hbx[:, h:h + 1])\
                   .then_inc(pair_free[e % 4], 1)
            for h in range(KD):
                act.wait_ge(p1_ready, h + 1)
                act.wait_ge(pair_free[(9 + h) % 4], f0[(9 + h) % 4] + (9 + h) // 4 + 1)
                act.activation(xc(h), yt(h), ACT.Tanh, scale=sp2[:, h:h + 1], bias=sp2[:, h:h + 1]).then_inc(t2_ready, 1)
                act.activation(yt(h), yt(h), ACT.Exp, scale=spm4[:, h:h + 1], bias=spm4[:, h:h + 1]).then_inc(a_ready, 1)
                if h % 4 == 3:
                    split_hi(n0 + 11 + h // 4)
            for h in range(KD):
                act.wait_ge(t2_ready, h + 1)
                act.activation(xc(h), xc(h), ACT.Sqrt, scale=0.25).then_inc(sqrt_ready, 1)
                if h == 5:
                    split_hi(n0 + 13)
            for v in range(1, KD):
                if v >= 6:
                    wide_hi("RO", v - 6)
                if 1 < v < KD - 2:
                    split_hi(n0 + 12 + v)
                y_gelu(v, 24 + v)

            out_phase("RO")
            ffn_in("FI1", "FO1")
            out_phase("FO1")

            p = POST["FO1"]
            act.wait_ge(unit_done, base["END"])
            y_out(p, 1, 1, 3)
            post_std(p, 1)
            act.wait_ge(so_turned, 1)
            act.activation(wide[0:36, NT * D:(NT + 1) * D], psf[0:36, 4 * BANK:6 * BANK], ACT.Copy).then_inc(so_copied, 1)
            post_rb(p, 1)
            for b in range(2 * NT):
                if out_by_act(b):
                    act.wait_ge(out_turned, b + 1)
                    act.activation(out_tile(b), out_bank(b), ACT.Copy).then_inc(out_act, 1)

        @block.vector
        def _(dve):
            def split_lo(n, width=1024, i=0, per=0):
                s = slot(n)
                dve.wait_ge(hi_ready, i * per + (n + 1))
                dve.tensor_tensor(wlo[:, s, 0:width], stage[:, s, 0:width], whi[:, s, 0:width].bitcast(F32),
                                  ALU.subtract).then_inc(lo_ready, 1)

            def width_of(n):
                for name in ("FO0", "FO1"):
                    if base[name] <= n < base[name] + 24 and (n - base[name]) % 12 < 2:
                        return 512
                return 1024

            def add_squares(j, r):
                if r == 0:
                    return
                if r >= 2:
                    dve.wait_ge(sq_added, 8 * j + r - 1)
                for part, at in enumerate([slice(0, TT)] if r < KD - 1 else [half(0), half(1)]):
                    dve.wait_ge(sq_ready, 9 * j + r + part + 1)
                    dve.tensor_tensor(acc[:, at], acc[:, at], tmp[:, r % 3, at], ALU.add).then_inc(sq_added, 1)

            def post_add(p, G, h, m):
                if (G, m) == (0, 0):
                    return
                dve.wait_ge(psq_ready, count_sq(p, G, h, m))
                if count_add(p, G, h, m) > 1:
                    dve.wait_ge(psq_added, count_add(p, G, h, m) - 1)
                r = 4 * G + m
                dve.tensor_tensor(acc[:, half(h)], acc[:, half(h)], tmp[:, r % 3, half(h)], ALU.add).then_inc(psq_added, 1)

            def diag_of(j):
                dve.wait_ge(std_ready, j + 1)
                dve.reciprocal(rtok[:, :], std[:, :]).then_inc(rtok_ready, 1)
                dve.wait_ge(rtok_ready, j + 1)
                dve.tensor_tensor(diag.rearrange("p (c t) -> p c t", c=NT),
                                  ident[:, :].unsqueeze(1).to_broadcast([P, NT, P]),
                                  bc3(rtok[:, :], P), ALU.mult).then_inc(diag_ready, 1)

            def post_diag(p, h):
                dve.wait_ge(pstd_ready, count_post(p, h))
                dve.reciprocal(prtok[0:CH, h, :], pstd[0:CH, h, :]).then_inc(prtok_ready, 1)
                dve.wait_ge(prtok_ready, count_post(p, h))
                dve.tensor_tensor(pdiag(h).rearrange("p (c t) -> p c t", c=3),
                                  ident[0:CH, 0:CH].unsqueeze(1).to_broadcast([CH, 3, CH]),
                                  bc3(prtok[0:CH, h, :], CH), ALU.mult).then_inc(pdiag_ready, 1)

            def h_low(k, layer, i, at, count):
                dve.wait_ge(h_hi, count)
                dve.scalar_tensor_tensor(hl[:, k, at], xT[:, k, at], gain(layer, i, k), hh[:, k, at].bitcast(F32),
                                         ALU.mult, ALU.subtract).then_inc(h_lo, 1)

            def wide_lo(name, s):
                units = out_units(name)
                j = s % len(units)
                k, nk = units[j]
                at = 2 * (j % 4)
                src0 = (GATE0 if name == "RO" else 0) + k * TT
                dve.wait_ge(a_hi, AB[name] + s + 1)
                dve.tensor_tensor(hl[:, at:at + nk, :].rearrange("p k n -> p (k n)"), wide[:, src0:src0 + nk * TT],
                                  hh[:, at:at + nk, :].rearrange("p k n -> p (k n)").bitcast(F32),
                                  ALU.subtract).then_inc(a_lo, 1)

            dve.memset(acc[:, TT:NT * P], 0.0)
            dve.wait_ge(x_turned, 1)
            dve.tensor_copy(xT[:, :, T:TT], ps[:, 7, :].rearrange("p (k n) -> p k n", k=KD)).then_inc(x_ready, 1)

            def x_tile(k):
                dve.wait_ge(x_turned, k + 2)
                dve.tensor_copy(xT[:, k, 0:T], ps[:, 5 + k % 2, :]).then_inc(x_ready, 1)

            x_tile(0)
            dve.wait_ge(par1_ready, 1)
            for k in range(KD):
                if k + 1 < KD:
                    x_tile(k + 1)
                if k < 2:
                    split_lo(k, 2 * GW)
                h_low(k, 0, 0, slice(0, TT), k + 1)
                add_squares(0, k)
                if k in (2, 4, 6):
                    split_lo(1 + k // 2, 2 * GW)
            split_lo(5, 2 * GW)
            diag_of(0)

            def v_evict(g, i=0):
                for t in range(NT):
                    if t < NC:
                        dve.wait_ge(v_tile_done, i * NC + (NC * g + t + 1))
                    else:
                        dve.wait_ge(unit_done, i * 4 + (4 * g + 4))
                    r = P if t < NC else TS
                    src = ps[0:r, t, 0:GW]
                    if t == NC and g > 0:
                        dve.wait_ge(vlow_out, i + g)
                        dve.tensor_tensor(vlow, vlow, src, ALU.add).then_inc(vlow_added, 1)
                        dve.wait_ge(vlow_added, i + g)
                        src = vlow
                    dve.scalar_tensor_tensor(z(i + g, t), src, rtok[0:r, t:t + 1],
                                             brow[0:r, bass.ds(i * GW + g * GW, GW)], ALU.mult, ALU.add)\
                       .then_inc(z_evicted, 1)

            def v_stats(g, i=0):
                for t in range(NT):
                    r = P if t < NC else TS
                    dve.wait_ge(z_act, i * NT + (NT * g + t + 1))
                    dve.bn_stats(stats[0:r, t, bass.ds(i + g, 1), :].rearrange("p a s -> p (a s)"), z(i + g, t))\
                       .then_inc(z_stats, 1)

            def v_group(g, i=0, last=False):
                for j in range(4):
                    split_lo(4 * g + j + 2, 1024 if last and j >= 2 else 2 * GW, i, 0 if last or g < 3 else 4)
                    if j == 1:
                        v_stats(g - 1, i)
                v_evict(g, i)

            def softplus():
                lam = par[:, LAM0:LAM0 + KD]
                w = [spw[:, j, :] for j in range(5)]
                n = [0]

                def step(ins):
                    ins.then_inc(sp_chain, 1)
                    n[0] += 1
                    dve.wait_ge(sp_chain, n[0])

                dve.wait_ge(par2_ready, 1)
                step(dve.tensor_scalar(w[0], lam, -1.0, None, ALU.mult))
                step(dve.tensor_tensor(w[1], w[0], lam, ALU.max))
                dve.wait_ge(sp_exp, 1)
                step(dve.tensor_scalar(w[3], w[2], 2.0, None, ALU.add))
                step(dve.reciprocal(w[4], w[3]))
                step(dve.tensor_tensor(w[3], w[2], w[4], ALU.mult))
                step(dve.tensor_tensor(w[4], w[3], w[3], ALU.mult))
                step(dve.tensor_scalar(w[1], w[4], 2.0 / 19, None, ALU.mult))
                for odd in range(17, 1, -2):
                    step(dve.scalar_tensor_tensor(w[1], w[1], 2.0 / odd, w[4], ALU.add, ALU.mult))
                step(dve.scalar_tensor_tensor(w[1], w[1], 2.0, w[3], ALU.add, ALU.mult))
                step(dve.scalar_tensor_tensor(w[2], w[0], 0.0, w[1], ALU.max, ALU.add))
                dve.tensor_scalar(sp2[:, :], w[2], 2.0, None, ALU.mult)
                dve.tensor_scalar(spm4[:, :], w[2], -4.0, None, ALU.mult).then_inc(sp_ready, 1)
                dve.tensor_scalar(hba[:, :], par[:, BA0:BA0 + KD], 0.5, None, ALU.mult)
                dve.tensor_scalar(hbx[:, :], par[:, BX0:BX0 + KD], 0.5, None, ALU.mult).then_inc(hb_ready, 1)

            dve.wait_ge(brow_landed, 16)
            v_evict(0)
            v_group(1)
            v_group(2)
            softplus()
            with dve.Fori(0, GRP - 4) as i:
                v_group(3, i)
            v_group(GRP - 1, last=True)
            v_stats(GRP - 1)
            for t in range(NT):
                r = P if t < NC else TS
                dve.wait_ge(z_stats, NT * (GRP - 1) + t + 1)
                last = dve.bn_aggr(mv[0:r, t, :], stats[0:r, t, :, :].rearrange("p g s -> p (g s)"))
            last.then_inc(var_ready, 1)
            dve.wait_ge(lnstd_ready, 1)
            dve.reciprocal(lnr[:, 0:NC], lnr[:, 0:NC])
            dve.reciprocal(lnr[0:TS, NC:NT], lnr[0:TS, NC:NT]).then_inc(ln_ready, 1)
            dve.wait_ge(ln_ready, 1)

            def center(b, i, first=False):
                if not first:
                    dve.wait_ge(mix_done, i * (2 * FG) + (b - 1) * FG)
                    dve.wait_ge(v_stored[b], i * 16)
                dve.wait_ge(lnrow_landed[b], i * 32 + 32)
                for t in range(NT):
                    r = P if t < NC else TS
                    dve.scalar_tensor_tensor(vbuf[b][0:r, t, :], z(i * 2 + b, t), mv[0:r, t, 0:1],
                                             lnrow[b][0:r, 0:GW], ALU.subtract, ALU.mult).then_inc(ln_half, 1)

            def scale(b, i):
                for t in range(NT):
                    r = P if t < NC else TS
                    dve.wait_ge(ln_half, i * (2 * NT) + (b * NT + t + 1))
                    dve.scalar_tensor_tensor(vbuf[b][0:r, t, :], vbuf[b][0:r, t, :], lnr[0:r, t:t + 1],
                                             lnrow[b][0:r, GW:2 * GW], ALU.mult, ALU.add).then_inc(ln_done, 1)

            def mix_evict(x, xs, g):
                dve.wait_ge(mix_done, x + 1)
                bs = bsrow[:, bass.ds(g, 1), :]
                dve.tensor_tensor(wideA[:, bass.ds(xs * TT, T)].rearrange("p (c t) -> p c t", c=NC),
                                  ps[:, 6, :].rearrange("p (c t) -> p c t", c=NC),
                                  bs.to_broadcast([P, NC, P]), ALU.add)
                dve.tensor_tensor(wideA[:, bass.ds(xs * TT + T, TS)].rearrange("p (b t) -> p b t", b=NB),
                                  ps[:, 7, 0:TS].rearrange("p (b t) -> p b t", b=NB),
                                  bs[:, :, 0:NS].to_broadcast([P, NB, NS]), ALU.add).then_inc(pair_free[3], 1)

            def times_rb(out, m):
                return dve.tensor_tensor(halves(out), pair(m), halves(rb[:, :]), ALU.mult)

            def u_body(i, first=False, last=False):
                for c in range(6):
                    n = base["U"] + c
                    split_lo(n + 2, 1024, i, 6)
                    if c % 3 == 0:
                        center(c // 3, i, first)
                    if c % 3 == 1:
                        scale(c // 3, i)
                    if last and c == 5:
                        mix_evict(i * 6 + 3, i * 6 + 3, i * 2 + 1)
                        wide_lo("GO", 0)
                        mix_evict(i * 6 + 4, i * 6 + 4, i * 2 + 1)
                        wide_lo("GO", 1)
                    dve.wait_ge(unit_done, i * 6 + (n + 1))
                    if not (first and c < 3):
                        dve.wait_ge(gated, i * 6 + (c - 2))
                    times_rb(tmp[:, c % 3, :], c % 3).then_inc(pair_free[c % 3], 1)
                    if not (first and c < 2 or last and c == 5):
                        mix_evict(i * 6 + (c - 2), i * 6 + (c - 2), i * 2 + (c - 2) // 3)

            dve.wait_ge(rb_ready, 1)
            dve.wait_ge(bs_landed, 16)
            u_body(0, first=True)
            with dve.Fori(1, GRP // 2 - 1) as i:
                u_body(i)
            u_body(GRP // 2 - 1, last=True)
            mix_evict(DG // P - 1, DG // P - 1, GRP - 1)

            def out_phase(name):
                per, p = len(out_units(name)), POST[name]
                for s in range(2 * per):
                    n = base[name] + s
                    if n + 2 < base["END"]:
                        split_lo(n + 2, width_of(n + 2))
                    if s + 2 < 2 * per:
                        wide_lo(name, s + 2)
                    if s % per == per - 1:
                        for h in range(2):
                            for m in range(4):
                                if s // per == 1 and h == 1 and m > 0:
                                    break
                                post_add(p, s // per, h, m)
                                if (s // per, h, m) == (1, 0, 3):
                                    post_diag(p, 0)
                                    normed(p, 0, 0, add=x0_ready if NEXT[name] else x_last[0])
                                    if NEXT[name]:
                                        normed(p, 0, 1)
                                        split_lo(n + 3)
                                        low(NEXT[name], 0, 0)
                if NEXT[name]:
                    normed(p, 0, 2)

            def low(name, h, k):
                h_low(k, *PRE_GAIN[name], half(h), count_h(name, h, k))

            def normed(p, h, k, add=None):
                if k == 0 or (h, k) == (0, 1):
                    dve.wait_ge(prb_ready if h or k else pbc_done, count_post(p, h))
                y, x = yt(k)[:, half(h)], xT[:, k, half(h)]
                dve.scalar_tensor_tensor(y, y, gain(*POST_GAIN[p], k), rb[:, half(h)] if h or k else PBC(0), ALU.mult, ALU.mult)\
                   .then_inc(t_ready, 1)
                if add:
                    dve.wait_ge(t_ready, count_t(p, h, k))
                    dve.tensor_tensor(x, x, y, ALU.add).then_inc(add, 1)

            def first_tiles(name):
                j, p, n = PRE[name], PRE[name] - 1, base[name]
                for k in range(1, 4):
                    normed(p, 0, k + 2)
                    low(name, 0, k)
                    post_add(p, 1, 1, k)
                normed(p, 0, 6)
                low(name, 0, 4)
                post_diag(p, 1)
                normed(p, 0, 7)
                low(name, 0, 5)
                split_lo(n + 3)
                low(name, 0, 6)
                normed(p, 1, 0)
                normed(p, 1, 1)
                low(name, 0, 7)
                for k in range(KD):
                    if k + 2 < KD:
                        normed(p, 1, k + 2)
                    low(name, 1, k)
                    add_squares(j, k)
                diag_of(j)
                split_lo(n + 4)
                dve.wait_ge(rb_ready, j + 1)

            def ffn_evict(name, i, c, gated0, first=False):
                n = base[name] + c
                dve.wait_ge(unit_done, i * 4 + (n + 1))
                if c < 2:
                    times_rb(wtile(i * 2 + c), c).then_inc(pair_free[c], 1)
                else:
                    if not first:
                        dve.wait_ge(ffn_gated, i * 2 + (gated0 + c - 3))
                    times_rb(tmp[:, c - 2, :], c).then_inc(pair_free[c], 1)

            def ffn_in(name, layer, out):
                first_tiles(name)
                n, nb, g0 = base[name], KF // 2, KF * layer
                for c in range(4):
                    if c == 3:
                        split_lo(n + 5)
                    ffn_evict(name, 0, c, g0, first=True)
                with dve.Fori(1, nb - 1) as i:
                    for c in range(4):
                        split_lo(n + c + 2, 1024, i, 4)
                        ffn_evict(name, i, c, g0)
                for c in range(4):
                    split_lo(n + 4 * (nb - 1) + c + 2)
                    if c == 3:
                        wide_lo(out, 0)
                        wide_lo(out, 1)
                    ffn_evict(name, nb - 1, c, g0)

            out_phase("GO")
            ffn_in("FI0", 0, "FO0")
            out_phase("FO0")

            first_tiles("RI")
            n0, f0 = base["RI"], free0["RI"]

            def conv(u):
                dve.wait_ge(tap0, u + 1)
                xs = xc(u)[:, T:TT].rearrange("p (b t) -> p b t", b=NB)
                for w in range(1, CW):
                    tap = par[:, CVW0 + w * KD + u:CVW0 + w * KD + u + 1]
                    if w > 1:
                        dve.wait_ge(tap_chain, 5 * u + 2 * w - 3)
                    dve.scalar_tensor_tensor(xc(u)[:, 0:T], xb_p(u, w), tap, xc(u)[:, 0:T], ALU.mult, ALU.add)\
                       .then_inc(tap_chain, 1)
                    if w > 1:
                        dve.wait_ge(tap_chain, 5 * u + 2 * w - 2)
                    dve.scalar_tensor_tensor(xs, xb_s(u)[:, :, w:w + NS], tap, xs, ALU.mult, ALU.add)\
                       .then_inc(tap_chain if w < CW - 1 else conv_done, 1)

            def with_root(h):
                dve.wait_ge(sqrt_ready, h + 1)
                dve.tensor_tensor(xbt(h), xbt(h), xc(h), ALU.mult).then_inc(rooted, 1)

            def head(h):
                dve.wait_ge(a_ready, h + 1)
                if h < 4:
                    dve.wait_ge(rooted, h + 1)
                else:
                    dve.wait_ge(rooted_by_pool, h - 3)
                dve.scalar_tensor_tensor(xbt(h), yt(h), 1.0, xbt(h), ALU.add, ALU.mult).then_inc(b_ready, 1)

            def scan(h):
                dve.wait_ge(seq_ready, h + 1)
                dve.tensor_tensor_scan(xc(h), yt(h), xbt(h), 0.0, ALU.mult, ALU.add).then_inc(scanned, 1)

            def y_evict(v, e):
                dve.wait_ge(unit_done, n0 + 8 + v + 1)
                if v >= 3:
                    dve.wait_ge(y_act, v - 2)
                times_rb(tmp[:, v % 3, :], e % 4).then_inc(pair_free[e % 4], 1)

            dve.wait_ge(pads_ready, 1)
            def x_evict(u):
                dve.wait_ge(unit_done, n0 + u + 1)
                m, s0 = u % 4, T - HT
                dve.tensor_tensor(xb_p(u, CW - 1, HT), ps[:, 2 * m, 0:HT], rb[:, 0:HT], ALU.mult)
                dve.tensor_tensor(xb_p(u, CW - 1 + HT, s0), ps[:, 2 * m + 1, 0:s0], rb[:, HT:T], ALU.mult)
                dve.tensor_tensor(xb_s(u)[:, :, CW - 1:], ps[:, 2 * m + 1, s0:HT].rearrange("p (b t) -> p b t", b=NB),
                                  rb[:, T:TT].rearrange("p (b t) -> p b t", b=NB), ALU.mult).then_inc(pair_free[m], 1)

            for u in range(4):
                x_evict(u)
                if u == 1:
                    split_lo(n0 + 5)
            for u, convs in ((4, (0, 1)), (5, (2, 3)), (6, (4,)), (7, (5,))):
                split_lo(n0 + u + 2)
                for c in convs:
                    conv(c)
                x_evict(u)
            split_lo(n0 + KD + 2)
            conv(6)
            y_evict(0, 8)
            conv(7)
            for h in range(KD):
                e = 9 + KD + h
                dve.wait_ge(pair_free[e % 4], f0[e % 4] + e // 4 + 1)
                dve.scalar_tensor_tensor(xbt(h), xbt(h), 1.0, xc(h), ALU.add, ALU.mult).then_inc(p1_ready, 1)
            split_lo(n0 + 11)
            split_lo(n0 + 12)
            with_root(0)
            for v in range(1, 6):
                y_evict(v, 24 + v)
                split_lo(n0 + 12 + v)
                if v < 4:
                    with_root(v)
                if v < 5:
                    head(v - 1)
                if v >= 2:
                    scan(v - 2)
            wide_lo("RO", 0)
            y_evict(6, 30)
            head(4)
            head(5)
            scan(4)
            head(6)
            y_evict(7, 31)
            wide_lo("RO", 1)
            scan(5)
            for h in range(7, KD):
                head(h)
                scan(h - 1)
            scan(KD - 1)

            out_phase("RO")
            ffn_in("FI1", 1, "FO1")
            out_phase("FO1")
            p = POST["FO1"]
            for h in range(2):
                for k in range(KD):
                    if h or k:
                        normed(p, h, k, add=x_last[0] if x_by_dve(k) else None)
                    if h == 0 and k in (1, 2, 3):
                        post_add(p, 1, 1, k)
                    if (h, k) == (0, 4):
                        post_diag(p, 1)
            for b in range(2 * NT):
                if not out_by_act(b):
                    dve.wait_ge(out_turned, b + 1)
                    dve.tensor_copy(out_tile(b), out_bank(b)).then_inc(out_dve, 1)

        @block.gpsimd
        def _(pool):
            pool.memset(ident[:, :], 0.0).then_inc(consts, 1)
            pool.wait_ge(consts, 1)
            pool.affine_select(out=ident[:, :], in_=ident[:, :], compare_op=ALU.not_equal, fill=1.0,
                               base=0, pattern=[[-1, P]], channel_multiplier=1).then_inc(consts, 1)
            pool.memset(epsc[:, :], EPS)
            pool.memset(ones[:, :], 1.0).then_inc(consts, 1)
            pool.memset(wsblk[:, :, :], 0.0)
            pool.wait_ge(ws_landed, 16)
            pool.affine_select(out=wraw, in_=wraw, compare_op=ALU.is_ge, fill=0.0,
                               base=0, pattern=[[0, GRP], [-1, P]], channel_multiplier=1).then_inc(ws_masked, 1)

            def ln_rows(b, g):
                for j, v in enumerate((gm_ln_g, gm_ln_b)):
                    pool.dma_start(lnrow[b][:, j * GW:(j + 1) * GW],
                                   v[0, bass.ds(g * GW, GW)].partition_broadcast(P)).then_inc(lnrow_landed[b], 16)

            pool.wait_ge(ws_ready, 2)
            for b in range(NB):
                pool.dma_start(wsblk[NS * b:NS * (b + 1), :, NS * b:NS * (b + 1)], wsT[0:NS, :, 0:NS])\
                    .then_inc(blk_landed, 16)
            ln_rows(0, 0)
            ln_rows(1, 1)

            def gate_u(x, i):
                pool.wait_ge(u_act, i * 6 + (x + 1))
                pool.wait_ge(pair_free[3], i * 6 + (x + 1))
                w = wtile(i * 6 + x)
                pool.tensor_tensor(w, w, tmp[:, x % 3, :], ALU.mult).then_inc(gated, 1)

            def u_body(i, last=False):
                for c in range(6):
                    if c % 3 == 0:
                        b = c // 3
                        pool.wait_ge(ln_done, i * (2 * NT) + (b + 1) * NT)
                        pool.dma_start(s_v[0].rearrange("b t e -> (b t) e")[:, bass.ds(i * (2 * GW) + b * GW, GW)],
                                       vbuf[b][0:TS, NC, :]).then_inc(v_stored[b], 16)
                        if not last:
                            ln_rows(b, i * 2 + (b + 2))
                    gate_u(c, i)

            with pool.Fori(0, GRP // 2 - 1) as i:
                u_body(i)
            u_body(GRP // 2 - 1, last=True)

            def residual(p):
                for h in range(2):
                    for k in range(KD):
                        if h or k:
                            x = xT[:, k, half(h)]
                            pool.wait_ge(t_ready, count_t(p, h, k))
                            pool.tensor_tensor(x, x, yt(k)[:, half(h)], ALU.add).then_inc(res_ready, 1)

            def ffn_gate(name, layer):
                with pool.Fori(0, KF // 2) as i:
                    for c in range(2):
                        pool.wait_ge(f_act, i * 2 + (KF * layer + c + 1))
                        pool.wait_ge(pair_free[2 + c], i + (free0[name][2 + c] + 1))
                        w = wtile(i * 2 + c)
                        pool.tensor_tensor(w, w, tmp[:, c, :], ALU.mult).then_inc(ffn_gated, 1)

            residual(0)
            ffn_gate("FI0", 0)
            pool.wait_ge(a_lo, AB["RO"])
            pool.wait_ge(par2_ready, 1)
            xall = wide[:, 0:KD * XB].rearrange("p (h n) -> p h n", h=KD)
            pool.memset(xall[:, :, 0:CW - 1], 0.0)
            for h in range(KD):
                last = pool.tensor_copy(xb_s(h)[:, :, 0:CW - 1],
                                        hist[:, h, 0:NB * (CW - 1)].rearrange("p (b w) -> p b w", b=NB))
            last.then_inc(pads_ready, 1)
            residual(1)
            f0 = free0["RI"]
            for u in range(KD):
                pool.wait_ge(pair_free[u % 4], f0[u % 4] + u // 4 + 1)
                tap, cb = par[:, CVW0 + u:CVW0 + u + 1], par[:, CVB0 + u:CVB0 + u + 1]
                pool.tensor_scalar(xc(u)[:, 0:T], xb_p(u, 0), tap, cb, ALU.mult, ALU.add)
                pool.tensor_scalar(xc(u)[:, T:TT].rearrange("p (b t) -> p b t", b=NB), xb_s(u)[:, :, 0:NS],
                                   tap, cb, ALU.mult, ALU.add).then_inc(tap0, 1)
                pool.tensor_copy(sout[:, u, 0:3], xb_p(u, T, CW - 1))
                pool.tensor_copy(sout[:, u, 3:27].rearrange("p (b w) -> p b w", b=NB), xb_s(u)[:, :, NS:])\
                    .then_inc(tails, 1)

            def gate_h(h):
                pool.wait_ge(scanned, h + 1)
                pool.wait_ge(y_act, h + 1)
                pool.tensor_copy(sout[:, h, 27:28], xc(h)[:, T - 1:T])
                pool.tensor_copy(sout[:, h, 28:36], xc(h)[:, T:TT].rearrange("p (b t) -> p b t", b=NB)[:, :, NS - 1])
                pool.tensor_tensor(gate(h), gate(h), xc(h), ALU.mult).then_inc(rg_gated, 1)

            for h in range(KD):
                pool.wait_ge(b_ready, h + 1)
                a0 = yt(h)[:, T:TT].rearrange("p (b t) -> p b t", b=NB)[:, :, 0]
                b0 = xbt(h)[:, T:TT].rearrange("p (b t) -> p b t", b=NB)[:, :, 0]
                pool.tensor_tensor(s8[:, h % 2, :], a0, hist[:, h, 24:32], ALU.mult).then_inc(pool_chain, 1)
                pool.wait_ge(pool_chain, 2 * h + 1)
                pool.tensor_tensor(b0, b0, s8[:, h % 2, :], ALU.add).then_inc(pool_chain, 1)
                pool.wait_ge(pool_chain, 2 * h + 2)
                pool.memset(a0, 0.0).then_inc(seq_ready, 1)
                if h < 4:
                    pool.wait_ge(sqrt_ready, h + 5)
                    pool.tensor_tensor(xbt(h + 4), xbt(h + 4), xc(h + 4), ALU.mult).then_inc(rooted_by_pool, 1)
                if h:
                    gate_h(h - 1)
            gate_h(KD - 1)
            residual(2)
            ffn_gate("FI1", 1)
            for h in range(2):
                for k in range(KD):
                    if not x_by_dve(k):
                        x = xT[:, k, half(h)]
                        pool.wait_ge(t_ready, count_t(POST["FO1"], h, k))
                        pool.tensor_tensor(x, x, yt(k)[:, half(h)], ALU.add).then_inc(x_last[1], 1)


_INS = ["x_prompt", "x_sample", "state_conv", "state_h", "norm_gains",
        "gm_w_in", "gm_b_in", "gm_ln_g", "gm_ln_b", "gm_w_s", "gm_b_s", "gm_w_out",
        "rg_w_in", "rg_conv_w", "rg_conv_b", "rg_w_a", "rg_b_a", "rg_w_x", "rg_b_x", "rg_lambda", "rg_w_out",
        "ffn_w_in", "ffn_w_out"]


def kernel(**inputs):
    import numpy as _np
    import concourse.bacc as _bacc
    from concourse import mybir as _mybir
    from concourse.bass_utils import run_bass_kernel_spmd as _run

    shape = {n: tuple(inputs[n].shape) for n in _INS}
    B, T, D = shape["x_prompt"]
    NBS, TSS, _ = shape["x_sample"]
    L, _, W, _ = shape["state_conv"]
    outs = [(B, T, D), (NBS, TSS, D), (L, B, W, D), (L, B, D), (L, NBS, W, D), (L, NBS, D),
            (shape["gm_ln_g"][0], NBS, TSS, shape["gm_ln_g"][1])]
    nc = _bacc.Bacc("TRN2", target_bir_lowering=False, num_devices=1, dynamic_dma_scratch_size=4096)
    arrays, args = {}, []
    for name in _INS:
        a = _np.ascontiguousarray(inputs[name])
        arrays[f"in_{name}_dram"] = a
        args.append(nc.dram_tensor(f"in_{name}_dram", a.shape, _mybir.dt.from_np(a.dtype), kind="ExternalInput").ap())
    for i, s in enumerate(outs):
        args.append(nc.dram_tensor(f"out_{i}_dram", s, _mybir.dt.float32, kind="ExternalOutput").ap())
    trunk_kernel(nc, *args)
    r = _run(nc, [arrays], core_ids=[0])
    return tuple(r.results[0][f"out_{i}_dram"] for i in range(len(outs)))
```
